# Optimizing a Trainium2 kernel written in Bass

```python
import math
import jax, jax.numpy as jnp
from jax import lax
import numpy as np

D_MODEL = 1024
BATCH = 1
SEQ = 256
DEPTH = 2

N_MEM = 256
HEAD_DIM = 64
MEM_HEADS = 4
MEM_WIDTH = MEM_HEADS * HEAD_DIM
MAIN_WIDTH = D_MODEL - MEM_WIDTH

GLA_HEADS = 4
GLA_DV = MAIN_WIDTH // GLA_HEADS
GLA_DK = GLA_DV // 2
GLA_LOWRANK = 16
GLA_TAU = 16.0
GLA_CHUNK = 64

SWA_HEADS = MAIN_WIDTH // HEAD_DIM
SWA_KV_HEADS = 4
WINDOW = 128
ROPE_DIM = HEAD_DIM // 4
ROPE_THETA = 500000.0

D_FF = 2816
N_EXPERTS = 8
TOP_K = 2
D_FF_EXPERT = 3584

EPS = 1e-6
N_LAYERS_A = (DEPTH + 1) // 2
N_LAYERS_B = DEPTH // 2

W_IN_A = 2 * GLA_HEADS * GLA_DK + MAIN_WIDTH + GLA_LOWRANK + MAIN_WIDTH + MEM_WIDTH
W_IN_B = SWA_HEADS * HEAD_DIM + 2 * SWA_KV_HEADS * HEAD_DIM + MEM_WIDTH

kernel_name = "hybrid_gla_swa_sink_memxattn_moe"

def rms_norm(x, gain):
    xf = x.astype(jnp.float32)
    y = xf * lax.rsqrt(jnp.mean(xf * xf, axis=-1, keepdims=True) + EPS)
    return (y * gain.astype(jnp.float32)).astype(x.dtype)

def partial_rope(t, positions):
    half = ROPE_DIM // 2
    inv_freq = jnp.power(jnp.float32(ROPE_THETA), -jnp.arange(half, dtype=jnp.float32) / half)
    ang = positions.astype(jnp.float32)[:, :, None] * inv_freq
    cos = jnp.cos(ang)[:, :, None, :]
    sin = jnp.sin(ang)[:, :, None, :]
    tf = t.astype(jnp.float32)
    x1 = tf[..., :half]
    x2 = tf[..., half:ROPE_DIM]
    out = jnp.concatenate([x1 * cos - x2 * sin, x2 * cos + x1 * sin, tf[..., ROPE_DIM:]], axis=-1)
    return out.astype(t.dtype)

def gla_chunked(q, k, v, log_alpha):
    B, S, H, dk = q.shape
    dv = v.shape[-1]
    C = GLA_CHUNK
    N = S // C

    def to_chunks(t):
        return t.astype(jnp.float32).reshape(B, N, C, H, t.shape[-1]).transpose(1, 0, 3, 2, 4)

    qc, kc, vc, gc = to_chunks(q), to_chunks(k), to_chunks(v), to_chunks(log_alpha)
    b = jnp.cumsum(gc, axis=3)
    b_last = b[:, :, :, -1:, :]
    q_dec = qc * jnp.exp(b)
    k_dec = kc * jnp.exp(-b)
    k_to_end = kc * jnp.exp(b_last - b)

    causal = jnp.tril(jnp.ones((C, C), dtype=bool))
    attn = jnp.einsum('nbhtd,nbhsd->nbhts', q_dec, k_dec)
    attn = jnp.where(causal, attn, 0.0)
    o_intra = jnp.einsum('nbhts,nbhsv->nbhtv', attn, vc)

    chunk_kv = jnp.einsum('nbhsd,nbhsv->nbhdv', k_to_end, vc)
    chunk_decay = jnp.exp(b_last[:, :, :, 0, :])

    def step(state, inp):
        kv, dec = inp
        return dec[..., None] * state + kv, state

    state0 = jnp.zeros((B, H, dk, dv), jnp.float32)
    _, state_start = lax.scan(step, state0, (chunk_kv, chunk_decay))
    o_inter = jnp.einsum('nbhtd,nbhdv->nbhtv', q_dec, state_start)
    o = o_intra + o_inter
    return o.transpose(1, 0, 3, 2, 4).reshape(B, S, H, dv)

def sliding_window_gqa_sinks(q, k, v, sinks):
    B, S, H, D = q.shape
    Hkv = k.shape[2]
    G = H // Hkv
    W = WINDOW
    nb = S // W
    qb = q.reshape(B, nb, W, Hkv, G, D)

    def with_prev(t):
        cur = t.reshape(B, nb, W, Hkv, D)
        prev = jnp.concatenate([jnp.zeros_like(cur[:, :1]), cur[:, :-1]], axis=1)
        return jnp.concatenate([prev, cur], axis=2)

    kb, vb = with_prev(k), with_prev(v)
    s = jnp.einsum('bnqkgd,bnskd->bnkgqs', qb, kb).astype(jnp.float32) * (D ** -0.5)

    qi = jnp.arange(W)[:, None]
    kj = jnp.arange(2 * W)[None, :]
    dist = qi + W - kj
    band = (dist >= 0) & (dist < WINDOW)
    has_prev = (jnp.arange(nb)[:, None, None] > 0) | (kj >= W)[None]
    valid = (band[None] & has_prev)[None, :, None, None]

    sink = sinks.astype(jnp.float32).reshape(Hkv, G)[None, None, :, :, None]
    s = jnp.where(valid, s, -jnp.inf)
    m = jnp.maximum(jnp.max(s, axis=-1), sink)
    p = jnp.exp(s - m[..., None])
    denom = jnp.sum(p, axis=-1) + jnp.exp(sink - m)
    p = p / denom[..., None]
    out = jnp.einsum('bnkgqs,bnskd->bnqkgd', p.astype(vb.dtype), vb)
    return out.reshape(B, S, H * D)

def memory_cross_attention(qm, mem_n, w_mem_kv):
    B, S = qm.shape[:2]
    kv = mem_n @ w_mem_kv
    km = kv[..., :MEM_WIDTH].reshape(B, -1, MEM_HEADS, HEAD_DIM)
    vm = kv[..., MEM_WIDTH:].reshape(B, -1, MEM_HEADS, HEAD_DIM)
    s = jnp.einsum('bshd,bmhd->bhsm', qm, km).astype(jnp.float32) * (HEAD_DIM ** -0.5)
    p = jax.nn.softmax(s, axis=-1)
    out = jnp.einsum('bhsm,bmhd->bshd', p.astype(vm.dtype), vm)
    return out.reshape(B, S, MEM_WIDTH)

def swiglu(h, w_gate_up, w_down, d_ff):
    gu = h @ w_gate_up
    return (jax.nn.silu(gu[..., :d_ff]) * gu[..., d_ff:]) @ w_down

def moe_swiglu(h, router_w, exp_w_gate_up, exp_w_down):
    logits = (h @ router_w).astype(jnp.float32)
    top_v, top_i = lax.top_k(logits, TOP_K)
    gates = jax.nn.softmax(top_v, axis=-1)
    combine = jnp.sum(jax.nn.one_hot(top_i, N_EXPERTS, dtype=jnp.float32) * gates[..., None], axis=-2)
    y = jnp.zeros(h.shape, jnp.float32)
    for e in range(N_EXPERTS):
        y = y + combine[..., e:e + 1] * swiglu(h, exp_w_gate_up[e], exp_w_down[e], D_FF_EXPERT).astype(jnp.float32)
    return y.astype(h.dtype)

def setup_inputs(seed: int = 0) -> dict:
    key = jax.random.key(seed)
    ks = jax.random.split(key, 20)
    f32 = jnp.float32

    def w(k, shape, fan_in):
        return jax.random.normal(k, shape, f32) * (fan_in ** -0.5)

    def gain(k, shape):
        return 1.0 + 0.05 * jax.random.normal(k, shape, f32)

    x = jax.random.normal(ks[0], (BATCH, SEQ, D_MODEL), f32)
    mem = jax.random.normal(ks[1], (BATCH, N_MEM, D_MODEL), f32)
    offsets = jax.random.randint(ks[2], (BATCH, 1), 0, 4096, dtype=jnp.int32)
    positions = offsets + jnp.arange(SEQ, dtype=jnp.int32)[None, :]
    return {
        "x": x,
        "mem": mem,
        "positions": positions,
        "mix_norm": gain(ks[3], (DEPTH, D_MODEL)),
        "w_in_a": w(ks[4], (N_LAYERS_A, D_MODEL, W_IN_A), D_MODEL),
        "gla_gate_w": w(ks[5], (N_LAYERS_A, GLA_LOWRANK, GLA_HEADS * GLA_DK), GLA_LOWRANK),
        "gla_gate_b": 2.0 + 0.1 * jax.random.normal(ks[6], (N_LAYERS_A, GLA_HEADS * GLA_DK), f32),
        "gla_out_norm": gain(ks[7], (N_LAYERS_A, GLA_DV)),
        "w_in_b": w(ks[8], (N_LAYERS_B, D_MODEL, W_IN_B), D_MODEL),
        "swa_sinks": 0.5 * jax.random.normal(ks[9], (N_LAYERS_B, SWA_HEADS), f32),
        "mem_norm": gain(ks[10], (DEPTH, D_MODEL)),
        "w_mem_kv": w(ks[11], (DEPTH, D_MODEL, 2 * MEM_WIDTH), D_MODEL),
        "w_out": w(ks[12], (DEPTH, D_MODEL, D_MODEL), D_MODEL),
        "ffn_norm": gain(ks[13], (DEPTH, D_MODEL)),
        "ffn_w_gate_up": w(ks[14], (N_LAYERS_A, D_MODEL, 2 * D_FF), D_MODEL),
        "ffn_w_down": w(ks[15], (N_LAYERS_A, D_FF, D_MODEL), D_FF),
        "router_w": w(ks[16], (N_LAYERS_B, D_MODEL, N_EXPERTS), D_MODEL),
        "exp_w_gate_up": w(ks[17], (N_LAYERS_B, N_EXPERTS, D_MODEL, 2 * D_FF_EXPERT), D_MODEL),
        "exp_w_down": w(ks[18], (N_LAYERS_B, N_EXPERTS, D_FF_EXPERT, D_MODEL), D_FF_EXPERT),
        "final_norm": gain(ks[19], (D_MODEL,)),
    }

def reference(x, mem, positions, mix_norm, w_in_a, gla_gate_w, gla_gate_b, gla_out_norm,
              w_in_b, swa_sinks, mem_norm, w_mem_kv, w_out, ffn_norm, ffn_w_gate_up,
              ffn_w_down, router_w, exp_w_gate_up, exp_w_down, final_norm):
    B, S, _ = x.shape
    for i in range(DEPTH):
        j = i // 2
        h = rms_norm(x, mix_norm[i])
        mem_n = rms_norm(mem, mem_norm[i])
        if i % 2 == 0:
            z = h @ w_in_a[j]
            dqk = GLA_HEADS * GLA_DK
            o0 = 0
            q = z[..., o0:o0 + dqk]; o0 += dqk
            k = z[..., o0:o0 + dqk]; o0 += dqk
            v = z[..., o0:o0 + MAIN_WIDTH]; o0 += MAIN_WIDTH
            g_lr = z[..., o0:o0 + GLA_LOWRANK]; o0 += GLA_LOWRANK
            r = z[..., o0:o0 + MAIN_WIDTH]; o0 += MAIN_WIDTH
            qm = z[..., o0:o0 + MEM_WIDTH]
            gate_logits = (g_lr @ gla_gate_w[j] + gla_gate_b[j]).astype(jnp.float32)
            log_alpha = (jax.nn.log_sigmoid(gate_logits) / GLA_TAU).reshape(B, S, GLA_HEADS, GLA_DK)
            q = q.reshape(B, S, GLA_HEADS, GLA_DK) * (GLA_DK ** -0.5)
            k = k.reshape(B, S, GLA_HEADS, GLA_DK)
            v = v.reshape(B, S, GLA_HEADS, GLA_DV)
            o = gla_chunked(q, k, v, log_alpha)
            o = rms_norm(o, gla_out_norm[j]).reshape(B, S, MAIN_WIDTH)
            main = (o * jax.nn.silu(r.astype(jnp.float32))).astype(x.dtype)
        else:
            z = h @ w_in_b[j]
            dq = SWA_HEADS * HEAD_DIM
            dkv = SWA_KV_HEADS * HEAD_DIM
            q = z[..., :dq].reshape(B, S, SWA_HEADS, HEAD_DIM)
            k = z[..., dq:dq + dkv].reshape(B, S, SWA_KV_HEADS, HEAD_DIM)
            v = z[..., dq + dkv:dq + 2 * dkv].reshape(B, S, SWA_KV_HEADS, HEAD_DIM)
            qm = z[..., dq + 2 * dkv:]
            q = partial_rope(q, positions)
            k = partial_rope(k, positions)
            main = sliding_window_gqa_sinks(q, k, v, swa_sinks[j]).astype(x.dtype)
        mem_out = memory_cross_attention(qm.reshape(B, S, MEM_HEADS, HEAD_DIM), mem_n, w_mem_kv[i])
        mixed = jnp.concatenate([main, mem_out.astype(x.dtype)], axis=-1) @ w_out[i]
        x = x + mixed
        h = rms_norm(x, ffn_norm[i])
        if i % 2 == 0:
            x = x + swiglu(h, ffn_w_gate_up[j], ffn_w_down[j], D_FF)
        else:
            x = x + moe_swiglu(h, router_w[j], exp_w_gate_up[j], exp_w_down[j])
    return rms_norm(x, final_norm)


_drawn_inputs = setup_inputs


def setup_inputs(seed=0):
    import zlib

    import numpy as np

    out = dict(_drawn_inputs(seed))
    spreads = {}
    factors = {'swa_sinks': 4.684, 'mem_norm': 4.273}
    for name, (base, spread) in spreads.items():
        noise = np.random.default_rng([zlib.crc32(name.encode()), seed]).standard_normal(out[name].shape)
        drawn = base * np.exp(spread * noise) if base else spread * noise
        out[name] = __import__('jax').numpy.asarray(drawn.astype(out[name].dtype))
    for name, factor in factors.items():
        out[name] = (out[name] * factor).astype(out[name].dtype)
    return out
```

```python
import math
from contextlib import ExitStack

import numpy as np

import concourse.bass as bass
import concourse.mybir as mybir

F32 = mybir.dt.float32
F32R = mybir.dt.float32r
I32 = mybir.dt.int32
U32 = mybir.dt.uint32
ALU = mybir.AluOpType
ACT = mybir.ActivationFunctionType
AX = mybir.AxisListType

P = 128
D = 1024
KT = D // P
TOK = 256
TB = TOK // P
HD = 64
MEM_W = 256
MAIN_W = D - MEM_W
GH, GDV, GDK, LOWRANK = 4, 192, 96, 16
GQK = GH * GDK
GLA_TAU, GLA_CHUNK = 16.0, 64
WINDOW = 128
SH, SKV = 12, 4
ROPE_HALF = 8
ROPE_THETA = 500000.0
F_DENSE = 2816
F_STEP = 256
F_STEPS = F_DENSE // F_STEP
NE, F_EXP = 8, 3584
E_STEP = 512
E_STEPS = F_EXP // E_STEP
ROUNDS = TOK // P
EPS = 1e-6
MASKED = -1e30

RAW, SPLIT = 3, 6
UNIT = 2048

A_V, A_GLR, A_R, A_QM = 2 * GQK, 2 * GQK + MAIN_W, 2 * GQK + MAIN_W + LOWRANK, 2 * GQK + 2 * MAIN_W + LOWRANK
B_QK = (SH + SKV) * HD

U_KV0, U_A0, U_A1, U_KV1, U_A2, U_A3, U_A4, U_AQM = 0, 2, 4, 6, 8, 10, 12, 14
U_OUT0 = 15
U_FFN = 19
U_B0 = U_FFN + 3 * F_STEPS
U_B1, U_BV, U_BQM, U_OUT1 = U_B0 + 2, U_B0 + 4, U_B0 + 5, U_B0 + 6
U_EXP = U_OUT1 + 4
E_UNITS = 6 * E_STEPS
OUT_PAIRS = [3, 0, 1, 2]
Q_PAIRS = [(0, 3), (1, 4), (2, 5), (6, 9), (7, 10), (8, 11)]


def build(nc, x_in, mem_in, positions, mix_norm, w_in_a, gla_gate_w, gla_gate_b, gla_out_norm, w_in_b,
          swa_sinks, mem_norm, w_mem_kv, w_out, ffn_norm, ffn_w_gate_up, ffn_w_down, router_w,
          exp_w_gate_up, exp_w_down, final_norm, out):
    ctx = ExitStack()
    with ctx:
        place = [16512]

        def sb_at(name, shape, dt, offset):
            return nc.alloc_sbuf_tensor_at(name, shape, dt, offset=offset)

        def sb(name, shape, dt=F32):
            offset = place[0]
            place[0] += (int(np.prod(shape[1:])) * 4 + 31) // 32 * 32
            return sb_at(name, shape, dt, offset)

        def sem(name):
            return ctx.enter_context(nc.semaphore(name))

        raw = [sb(f"weights_raw{i}", [P, UNIT]) for i in range(RAW)]
        whi = [sb(f"weights_hi{i}", [P, UNIT], F32R) for i in range(SPLIT)]
        wlo = [sb(f"weights_lo{i}", [P, UNIT], F32R) for i in range(SPLIT)]
        x = sb("x", [P, TB, D])
        hT_at = place[0]
        hT = [sb("hT_hi", [P, KT, TOK], F32R), sb("hT_lo", [P, KT, TOK], F32R)]
        mT_at = place[0]
        mT = [sb("mT_hi", [P, KT, TOK], F32R), sb("mT_lo", [P, KT, TOK], F32R)]
        kmT = [sb(f"mem_kT{l}", [P, 2, TOK]) for l in range(2)]
        vm = [sb(f"mem_v{l}", [P, TB, MEM_W]) for l in range(2)]
        qmT = sb("mem_qT", [P, 2, TOK])
        ident = sb("ident", [P, P])
        cum_m = sb("cum_matrix", [P, P])
        rem_m = sb("rem_matrix", [P, P])
        causal = sb("causal_chunks", [P, P])
        before = sb("before_matrix", [P, P])
        ones = sb("ones", [P, P])
        window = sb("window_mask", [P, 3 * P])
        iota = sb("iota", [P, P])
        gains = sb("gains", [P, 48])
        gate_w_at = place[0]
        gate_w = sb("gate_w", [LOWRANK + 1, GQK])
        route = sb_at("route", [P, 256], F32, gate_w_at)
        gla_gain = sb("gla_gain", [P, GDV])
        router_raw = sb("router_raw", [P, KT, NE])
        router = [sb("router_hi", [P, KT, NE], F32R), sb("router_lo", [P, KT, NE], F32R)]
        sinks = sb("sinks", [P, SH])
        pos_i = sb("pos_i", [P, TB], I32)
        stats = sb("stats", [P, 64])
        rope_c = sb("rope_c", [P, 8, TB * ROPE_HALF])
        swa = sb("swa_stats", [P, 4, TB * SH])
        small = sb("small", [P, 64])
        route_u = sb("route_u", [P, TB, 8], U32)
        rounds_i = sb("rounds_i", [1, 1], I32)
        E0 = place[0]
        xn = sb_at("xn", [P, TB, D], F32, E0)
        z = sb_at("gla_z", [P, TB, A_QM], F32, E0)
        E1 = E0 + TB * A_QM * 4
        memn = sb_at("memn", [P, TB, D], F32, E1)
        gain_rows = sb_at("gain_rows", [48, P], F32, E1 + 8192)
        ex = [sb_at(f"gla_exp{i}", [P, TB, GQK], F32, E1 + i * 3072) for i in range(3)]
        attn = sb_at("gla_attn", [P, TB, GH, P], F32, E1)
        glrT = sb_at("gla_lowrankT", [LOWRANK + 1, TOK], F32, mT_at + 8192 + 7168)
        la = sb_at("gla_log_alpha", [P, TB, GQK], F32, mT_at + 8192 + 3072)
        abs_g = sb_at("gla_abs_gate", [P, TB, GQK], F32, mT_at)
        ln_g = sb_at("gla_ln_gate", [P, TB, GQK], F32, mT_at + 3072)
        state = [sb_at(f"gla_state{i}", [GDK, GH, GDV], F32, mT_at + a) for i, a in enumerate((0, 3072, 8192))]
        mp = sb_at("mem_probs", [P, TB, 2, 2, TOK], F32, hT_at)
        mpT = sb_at("mem_probsT", [P, 2, 2, TB, TOK], F32, hT_at + 8192)
        squares = sb_at("gla_squares", [P, GH, GDV], F32, hT_at + 8192)
        qdT = sb_at("gla_qT", [GDK, TB, GH, P], F32, hT_at)
        kdT = sb_at("gla_kT", [GDK, TB, GH, P], F32, hT_at + 4096)
        f_silu = [sb_at(f"ffn_silu{i}", [P, 2 * TOK], F32, E0 + 8192 + i * 2048) for i in range(2)]
        f_act = [sb_at(f"ffn_act{i}", [P, 2 * TOK], F32, E0 + 12288 + i * 2048) for i in range(2)]
        f_aT = [[sb_at(f"ffn_aT{i}_{h}", [P, 2, TOK], F32R, E0 + 16384 + i * 4096 + h * 2048) for h in range(2)]
                for i in range(2)]
        qk = sb_at("swa_qk", [P, TB, SH + SKV, HD], F32, E0)
        v_sb = vm[0]
        S = sb_at("swa_scores", [P, SH, 3 * P], F32, E0 + 8192)
        rope = [sb_at(f"rope{i}", [P, TB, SH + SKV, ROPE_HALF], F32, E0 + 8192 + i * 1024) for i in range(4)]
        qkT = sb_at("swa_qkT", [P, KT, TOK], F32, hT_at)
        spT = [sb_at(f"swa_probsT{i}", [P, 3 * P], F32, E0 + i * 1536) for i in range(4)]
        pick = sb_at("pick", [P, TB, P], F32, E0 + 8192)
        pickT = sb_at("pickT", [P, TOK], F32R, E0 + 9216)
        e_silu = sb_at("expert_silu", [P, E_STEP], F32, E0 + 10240)
        e_act = sb_at("expert_act", [P, E_STEP], F32, E0 + 12288)
        e_aT = [hT[h][:, 0:4, P:TOK] for h in range(2)]
        y_s = [mT[h][:, 0:4, :].rearrange("p a b -> p (a b)") for h in range(2)]
        final_gain = sb_at("final_gain", [P, D], F32, mT_at + 8192 + 4096)
        out_sb = sb_at("out_sb", [P, TB, D], F32, E0 + 14336)
        assert E1 + 9216 <= 229368, E0

        o_sb = z[:, :, 0:MAIN_W].rearrange("p t (h v) -> p t h v", h=GH)
        bank = [ctx.enter_context(nc.psum_tensor(f"bank{i}", [P, 512], F32)) for i in range(8)]

        x_loaded, mem_loaded, params_loaded = sem("x_loaded"), sem("mem_loaded"), sem("params_loaded")
        final_gain_loaded = sem("final_gain_loaded")
        out_written = sem("out_written")
        weights_landed = [sem(f"weights_landed{i}") for i in range(RAW)]
        weights_hi, weights_lo, weights_used = sem("weights_hi"), sem("weights_lo"), sem("weights_used")
        consts = sem("consts")
        pool_chain, act_chain, dve_chain = sem("pool_chain"), sem("act_chain"), sem("dve_chain")
        gains_turned, gains_ready = sem("gains_turned"), sem("gains_ready")
        root_ready = sem("root_ready")
        normed = sem("normed")
        turned = sem("turned")
        turned_hi, turned_lo = sem("turned_hi"), sem("turned_lo")
        kv_act, kv_dve = sem("kv_act"), sem("kv_dve")
        proj_act, proj_dve = sem("proj_act"), sem("proj_dve")
        mscore, mmax, mprob, mnorm = sem("mem_scores"), sem("mem_max"), sem("mem_probs"), sem("mem_norm")
        mturn, mturned = sem("mem_probs_turned"), sem("mem_probsT_ready")
        mout, mout_hi, mout_lo = sem("mem_out"), sem("mem_out_hi"), sem("mem_out_lo")
        glr_turned, glr_ready, gate_logits = sem("glr_turned"), sem("glr_ready"), sem("gate_logits")
        ln_ready, la_ready = sem("ln_ready"), sem("la_ready")
        cum_done, gexp = sem("cum_done"), sem("gla_exps")
        decay_done, decay_ready = sem("decay_done"), sem("decay_ready")
        gdec, gturn, gturned = sem("gla_decayed"), sem("gla_qk_turned"), sem("gla_qkT_ready")
        gattn, gattn_ready = sem("gla_attn_done"), sem("gla_attn_ready")
        gkv, gstate = sem("gla_kv"), sem("gla_state")
        go, go_act, go_dve = sem("gla_o_done"), sem("gla_o_act"), sem("gla_o_dve")
        silu_r, oroot, onorm = sem("silu_r"), sem("gla_o_root"), sem("gla_o_normed")
        mainT, mainT_hi, mainT_lo = sem("mainT"), sem("mainT_hi"), sem("mainT_lo")
        y_act, y_dve = sem("y_act"), sem("y_dve")
        f_silu_ready, f_act_ready = sem("ffn_silu_ready"), sem("ffn_act_ready")
        f_hi, f_lo = sem("ffn_aT_hi"), sem("ffn_aT_lo")
        angles, sincos, roped = sem("angles"), sem("sincos"), sem("roped")
        sturn, sturned_a, sturned_d = sem("swa_turn"), sem("swa_turned_act"), sem("swa_turned_dve")
        sscore, sscaled = sem("swa_scores"), sem("swa_scaled")
        smax, sprob, snorm, ssink = sem("swa_max"), sem("swa_probs"), sem("swa_normed"), sem("swa_sink")
        spturn, spturned_a, spturned_d = sem("swa_pT"), sem("swa_pT_act"), sem("swa_pT_dve")
        sout = sem("swa_out")
        router_hi, router_lo, logits = sem("router_hi"), sem("router_lo"), sem("logits")
        gap_ready, gap_exp = sem("gap_ready"), sem("gap_exp")
        mask_ready, ranks, routed = sem("mask_ready"), sem("ranks"), sem("routed")
        pick_made, pick_turned, pickT_ready = sem("pick_made"), sem("pick_turned"), sem("pickT_ready")
        gathered, gath_hi, gath_lo = sem("gathered"), sem("gathered_hi"), sem("gathered_lo")
        e_silu_ready, e_act_ready = sem("expert_silu"), sem("expert_act")
        e_turned, e_hi, e_lo = sem("expert_turned"), sem("expert_aT_hi"), sem("expert_aT_lo")
        e_y_hi, e_y_lo = sem("expert_y_hi"), sem("expert_y_lo")
        scattered, x_added = sem("scattered"), sem("x_added")

        def tiles(ap, k0, nk, c0, w):
            return ap[k0 * P:(k0 + nk) * P, c0:c0 + w].rearrange("(k p) c -> p k c", p=P)

        wa, wb, wo = w_in_a[0], w_in_b[0], [w_out[0], w_out[1]]
        wgu, wdn = ffn_w_gate_up[0], ffn_w_down[0]
        halves = lambda ap, c0, w: [tiles(ap, 0, 4, c0, w), tiles(ap, 4, 4, c0, w)]
        units = halves(w_mem_kv[0], 0, 512)
        units += halves(wa, 1536, 512) + halves(wa, 0, 512) + halves(w_mem_kv[1], 0, 512)
        units += halves(wa, 512, 512) + halves(wa, 1024, 512) + halves(wa, 2048, A_QM - 2048)
        units += [tiles(wa, 0, 8, A_QM, MEM_W)]
        units += [tiles(wo[0], 2 * p, 2, 0, D) for p in OUT_PAIRS]
        assert len(units) == U_FFN
        ffn_gu = [tiles(wgu, 0, 8, 0, F_STEP), tiles(wgu, 0, 8, F_DENSE, F_STEP)]
        tail = halves(wb, 0, 512) + halves(wb, 512, 512)
        tail += [tiles(wb, 0, 8, B_QK, SKV * HD), tiles(wb, 0, 8, B_QK + SKV * HD, MEM_W)]
        tail += [tiles(wo[1], 2 * p, 2, 0, D) for p in OUT_PAIRS]
        assert U_B0 + len(tail) == U_EXP

        def unit_view(buf, nk, w):
            return buf[:, 0:nk * w].rearrange("p (k c) -> p k c", k=nk)

        def size(n):
            return 4 * (A_QM - 2048) if U_A4 <= n < U_AQM else UNIT

        def qk_pieces(t, half, b):
            src = b[:].rearrange("p (h d) -> p h d", d=HD)
            if half == 0:
                return [(qk[:, t, 0:6].rearrange("p (j r) d -> p r j d", r=2),
                         src[:, 0:6].rearrange("p (r j) d -> p r j d", r=2)), (qk[:, t, 6:9:2], src[:, 6:8])]
            return [(qk[:, t, 10:11], src[:, 0:1]), (qk[:, t, 7:12:2], src[:, 1:4]), (qk[:, t, 12:16], src[:, 4:8])]

        block = ctx.enter_context(nc.Block())

        @block.sync
        def _(sp):
            sp.dma_start(memn[:], mem_in[0].rearrange("(t p) d -> p t d", p=P)).then_inc(mem_loaded, 16)
            sp.dma_start(x[:], x_in[0].rearrange("(t p) d -> p t d", p=P)).then_inc(x_loaded, 16)

            def load(n, slot_n, src):
                nk, w = src.shape[1], src.shape[2]
                if not isinstance(n, int) or n >= RAW:
                    sp.wait_ge(weights_lo, n - RAW + 1)
                sp.dma_start(unit_view(raw[slot_n % RAW], nk, w), src).then_inc(weights_landed[slot_n % RAW], 16)

            for n, src in enumerate(units):
                load(n, n, src)
            load(U_FFN, U_FFN, ffn_gu[0])
            load(U_FFN + 1, U_FFN + 1, ffn_gu[1])
            with sp.Fori(1, F_STEPS) as j:
                n = U_FFN - 1 + j * 3
                cols = bass.ds(j * F_STEP, F_STEP)
                load(n, U_FFN + 2, wgu[:, cols].rearrange("(k p) c -> p k c", p=P))
                cols = bass.ds(j * F_STEP + F_DENSE, F_STEP)
                load(n + 1, U_FFN + 3, wgu[:, cols].rearrange("(k p) c -> p k c", p=P))
                rows = wdn.rearrange("(j k p) c -> j p k c", p=P, k=2)
                load(n + 2, U_FFN + 4, rows[j - 1])
            load(U_B0 - 1, U_B0 - 1, wdn[F_DENSE - F_STEP:F_DENSE, :].rearrange("(k p) c -> p k c", p=P))
            for i, src in enumerate(tail):
                load(U_B0 + i, U_B0 + i, src)

            down = exp_w_down[0].rearrange("e (j u k p) c -> e j u p k c", u=2, k=2, p=P)

            def load_experts(r):
                with sp.Fori(0, NE) as e:
                    base = sp.snap(e * E_UNITS + (r * NE * E_UNITS + U_EXP))

                    def gate_up(n, slot_n, j):
                        for i, (c0, k0) in enumerate(((0, 0), (0, 4), (F_EXP, 0), (F_EXP, 4))):
                            cols = bass.ds(j * E_STEP + c0, E_STEP)
                            src = exp_w_gate_up[0, e, k0 * P:(k0 + 4) * P, cols]
                            load(n + i, slot_n + i, src.rearrange("(k p) c -> p k c", p=P))

                    gate_up(base, U_EXP, 0)
                    with sp.Fori(1, E_STEPS) as j:
                        n = sp.snap(base + j * 6 - 2)
                        gate_up(n, U_EXP + 4, j)
                        load(n + 4, U_EXP + 8, down[e, j - 1, 0])
                        load(n + 5, U_EXP + 9, down[e, j - 1, 1])
                    load(base + (E_UNITS - 2), U_EXP + E_UNITS - 2, down[e, E_STEPS - 1, 0])
                    load(base + (E_UNITS - 1), U_EXP + E_UNITS - 1, down[e, E_STEPS - 1, 1])

            load_experts(0)
            sp.wait_ge(routed, 1)
            rounds = sp.value_load(rounds_i[0:1, 0:1], min_val=1, max_val=ROUNDS)
            with sp.If(rounds > 1):
                load_experts(1)

            sp.wait_ge(normed, 6)
            sp.dma_start(out[0].rearrange("(t p) d -> p t d", p=P), out_sb[:]).then_inc(out_written, 16)
            sp.wait_ge(out_written, 16)

        @block.gpsimd
        def _(pool):
            count = [0]

            def then(ins):
                count[0] += 1
                ins.then_inc(pool_chain, 1)
                pool.wait_ge(pool_chain, count[0])

            for i, g in enumerate((mix_norm, mem_norm, ffn_norm)):
                pool.dma_start(gain_rows[16 * i:16 * i + 16, :],
                               g.rearrange("l (k p) -> (l k) p", p=P)).then_inc(params_loaded, 16)
            pool.dma_start(gate_w[0:LOWRANK, :], gla_gate_w[0]).then_inc(params_loaded, 16)
            pool.dma_start(gate_w[LOWRANK:LOWRANK + 1, :], gla_gate_b).then_inc(params_loaded, 16)
            pool.dma_start(gla_gain[:], gla_out_norm.partition_broadcast(P)).then_inc(params_loaded, 16)
            pool.dma_start(sinks[:], swa_sinks.partition_broadcast(P)).then_inc(params_loaded, 16)
            pool.dma_start(router_raw[:], router_w[0].rearrange("(k p) e -> p k e", p=P)).then_inc(params_loaded, 16)
            pool.dma_start(pos_i[:], positions[0].rearrange("(t p) -> p t", p=P),
                           allow_slow_non_contiguous=True).then_inc(params_loaded, 16)

            def select(ap, keep, fill, base, cm, step):
                n = ap.shape[1]
                then(pool.affine_select(out=ap, in_=ap, compare_op=keep, fill=fill, base=base,
                                        pattern=[[step, n]], channel_multiplier=cm))

            then(pool.memset(ident[:], 0.0))
            select(ident[:], ALU.not_equal, 1.0, 0, 1, -1)
            then(pool.memset(cum_m[:], 1.0 / GLA_TAU))
            select(cum_m[:], ALU.is_ge, 0.0, 0, -1, 1)
            then(pool.memset(cum_m[0:GLA_CHUNK, GLA_CHUNK:P], 0.0))
            then(pool.memset(rem_m[:], 1.0 / GLA_TAU))
            select(rem_m[:], ALU.is_ge, 0.0, -1, 1, -1)
            then(pool.memset(rem_m[GLA_CHUNK:P, 0:GLA_CHUNK], 0.0))
            then(pool.memset(causal[:], 1.0))
            select(causal[:], ALU.is_ge, 0.0, 0, -1, 1)
            then(pool.memset(causal[0:GLA_CHUNK, GLA_CHUNK:P], 0.0))
            then(pool.memset(before[:], 1.0))
            select(before[:], ALU.is_ge, 0.0, -1, -1, 1)
            then(pool.memset(window[:], 0.0))
            select(window[:, 0:P], ALU.is_ge, MASKED, 0, 1, -1)
            select(window[:, P:2 * P], ALU.is_ge, MASKED, -1, -1, 1)
            select(window[:, 2 * P:3 * P], ALU.is_ge, MASKED, 0, 1, -1)
            then(pool.iota(iota[:], pattern=[[1, P]], base=0, channel_multiplier=0,
                           allow_small_or_imprecise_dtypes=True))
            pool.memset(ones[:], 1.0).then_inc(consts, 1)

        @block.tensor
        def _(pe):
            mm = nc.tensor.matmul
            tr = nc.tensor.transpose

            def passes(psum, st, mv, first, last):
                mm(psum, st[0], mv[0], start=first, stop=False)
                mm(psum, st[1], mv[0], start=False, stop=False)
                return mm(psum, st[0], mv[1], start=False, stop=last)

            def unit(n, nk, w, m=0):
                pe.wait_ge(weights_lo, m * 6 + (n + 1))
                return [unit_view(b[n % SPLIT], nk, w) for b in (whi, wlo)]

            def to_T(src, call, waits):
                for b in range(4):
                    waits(b)
                    for k in (2 * b, 2 * b + 1):
                        for t in range(TB):
                            c = (k % 2) * TOK + t * P
                            ins = tr(bank[4 + b][:, c:c + P], src[:, t, k * P:(k + 1) * P], ident[:])
                    ins.then_inc(turned, 1)

            def project(n, k0, nk, w, st, banks, first, last, c0=0, cw=None):
                u = unit(n, nk, w)
                cw = w if cw is None else cw
                for k in range(nk):
                    for t in range(TB):
                        s = [a[:, k0 + k, t * P:(t + 1) * P] for a in st]
                        ins = passes(bank[banks[t]][:, 0:cw], s, [a[:, k, c0:c0 + cw] for a in u],
                                     first and k == 0, last and k == nk - 1)
                return ins

            def chunk(n, w, banks):
                project(n, 0, 4, w, hT, banks, True, False).then_inc(weights_used, 1)
                project(n + 1, 4, 4, w, hT, banks, False, True).then_inc(weights_used, 1)

            def mem_kv(n, banks):
                for h in range(2):
                    u = unit(n + h, 4, 512)
                    for k in range(4):
                        first, last = h == 0 and k == 0, h == 1 and k == 3
                        mem_k = [a[:, 4 * h + k, :] for a in mT]
                        for i in range(2):
                            passes(bank[banks[i]][:, 0:TOK], [a[:, k, i * P:(i + 1) * P] for a in u], mem_k,
                                   first, last)
                        for t in range(TB):
                            ins = passes(bank[banks[2 + t]][:, 0:MEM_W], [a[:, t * P:(t + 1) * P] for a in mem_k],
                                         [a[:, k, MEM_W:2 * MEM_W] for a in u], first, last)
                    ins.then_inc(weights_used, 1)

            def mem_query(n, banks):
                u = unit(n, KT, MEM_W)
                for i in range(2):
                    for k in range(KT):
                        ins = passes(bank[banks[i]][:, 0:TOK], [a[:, k, i * P:(i + 1) * P] for a in u],
                                     [a[:, k, :] for a in hT], k == 0, k == KT - 1)
                ins.then_inc(weights_used, 1)

            def mem_attention(l, scores_free):
                scores_free()
                for t in range(TB):
                    for par in range(2):
                        for i in range(2):
                            r = slice(par * HD, (par + 1) * HD)
                            ins = mm(bank[1 + 2 * t + par][:, i * TOK:(i + 1) * TOK],
                                     qmT[r, i, t * P:(t + 1) * P], kmT[l][r, i, :], start=True, stop=True)
                    ins.then_inc(mscore, 1)
                for t in range(TB):
                    pe.wait_ge(mnorm, 2 * l + t + 1)
                    for par in range(2):
                        b = bank[(5, 6, 7, 0)[2 * t + par]]
                        for i in range(2):
                            for mb in range(TB):
                                c = (2 * i + mb) * P
                                ins = tr(b[:, c:c + P], mp[:, t, par, i, mb * P:(mb + 1) * P], ident[:])
                        ins.then_inc(mturn, 1)
                pe.wait_ge(mturned, 4 * l + 4)
                for par in range(2):
                    for i in range(2):
                        for mb in range(TB):
                            h = 2 * i + par
                            ins = mm(bank[1][par * HD:(par + 1) * HD, i * TOK:(i + 1) * TOK],
                                     vm[l][:, mb, h * HD:(h + 1) * HD], mpT[:, par, i, mb, :],
                                     start=(mb == 0), stop=(mb == TB - 1))
                ins.then_inc(mout, 1)

            def seed(b0):
                for t in range(TB):
                    for h in range(2):
                        mm(bank[b0 + 2 * t + h][:], ident[:], x[:, t, h * 512:(h + 1) * 512], start=True, stop=False)

            def rows_product(u, k_of, st, b0, last):
                for i in range(2):
                    for t in range(TB):
                        for h in range(2):
                            s = [a[:, k_of + i, t * P:(t + 1) * P] for a in st]
                            ins = passes(bank[b0 + 2 * t + h][:], s, [a[:, i, h * 512:(h + 1) * 512] for a in u],
                                         False, last and i == 1)
                return ins

            def project_out(n, l):
                seed(0)
                pe.wait_ge(mout_lo, l + 1)
                for i, pair in enumerate(OUT_PAIRS):
                    if i > 0:
                        pe.wait_ge(mainT_lo, 3 * l + pair + 1)
                    ins = rows_product(unit(n + i, 2, D), 2 * pair, mT, 0, i == 3)
                    ins.then_inc(weights_used, 1)

            pe.wait_ge(consts, 1)
            pe.wait_ge(params_loaded, 16 * 9)
            tr(bank[0][:, 0:48], gain_rows[:], ident[0:48, 0:48]).then_inc(gains_turned, 1)
            pe.wait_ge(normed, 1)
            to_T(memn, 0, lambda b: None)
            pe.wait_ge(gains_ready, 1)
            pe.wait_ge(turned_lo, 4)
            mem_kv(U_KV0, (0, 1, 2, 3))
            pe.wait_ge(normed, 2)
            to_T(xn, 1, lambda b: None)
            pe.wait_ge(turned_lo, 8)
            pe.wait_ge(kv_act, 1)
            chunk(U_A0, 512, (0, 1))
            to_T(memn, 2, lambda b: None)
            pe.wait_ge(kv_dve, 1)
            chunk(U_A1, 512, (2, 3))
            pe.wait_ge(turned_lo, 12)
            mem_kv(U_KV1, (4, 5, 6, 7))
            pe.wait_ge(proj_act, 1)
            pe.wait_ge(proj_dve, 1)
            chunk(U_A2, 512, (0, 1))

            pe.wait_ge(kv_act, 2)
            pe.wait_ge(kv_dve, 2)
            for t in range(TB):
                ins = tr(bank[4][0:LOWRANK, t * P:(t + 1) * P], z[:, t, A_GLR:A_GLR + LOWRANK], ident[:])
            ins.then_inc(glr_turned, 1)
            pe.wait_ge(proj_act, 2)
            pe.wait_ge(proj_dve, 2)
            chunk(U_A3, 512, (2, 3))
            pe.wait_ge(glr_ready, 1)
            for t in range(TB):
                ins = mm(bank[5 + t][:, 0:GQK], glrT[:, t * P:(t + 1) * P], gate_w[:], start=True, stop=True)
                ins.then_inc(gate_logits, 1)
            pe.wait_ge(proj_act, 3)
            pe.wait_ge(proj_dve, 3)
            chunk(U_A4, A_QM - 2048, (0, 1))
            for t in range(TB):
                pe.wait_ge(la_ready, t + 1)
                for i, m in enumerate((cum_m, rem_m)):
                    ins = mm(bank[(4, 7, 5, 6)[2 * t + i]][:, 0:GQK], m[:], la[:, t, :], start=True, stop=True)
                ins.then_inc(cum_done, 1)
            pe.wait_ge(proj_act, 4)
            pe.wait_ge(proj_dve, 4)
            mem_query(U_AQM, (2, 3))
            pe.wait_ge(proj_act, 5)
            pe.wait_ge(proj_dve, 5)
            for i, (t, r) in enumerate(((0, slice(GLA_CHUNK, P)), (1, slice(0, GLA_CHUNK)))):
                for h in range(GH):
                    ins = mm(bank[i][0:GDK, h:h + 1], la[r, t, h * GDK:(h + 1) * GDK],
                             cum_m[r, P - 1:P] if i == 0 else cum_m[r, GLA_CHUNK - 1:GLA_CHUNK],
                             start=True, stop=True)
            ins.then_inc(decay_done, 1)

            def free_a():
                pe.wait_ge(proj_act, 6)
                pe.wait_ge(proj_dve, 6)
                pe.wait_ge(gexp, 6)
                pe.wait_ge(decay_ready, 2)

            mem_attention(0, free_a)
            for t in range(TB):
                pe.wait_ge(gdec, 3 * t + 3)
                for i in range(2):
                    for h in range(GH):
                        ins = tr(bank[2 + 2 * t + i][0:GDK, h * P:(h + 1) * P],
                                 z[:, t, i * GQK + h * GDK:i * GQK + (h + 1) * GDK], ident[:])
                    ins.then_inc(gturn, 1)
            for t in range(TB):
                pe.wait_ge(gturned, 2 * t + 2)
                for h in range(GH):
                    ins = mm(bank[6 + t][:, h * P:(h + 1) * P], kdT[:, t, h, :], qdT[:, t, h, :], start=True, stop=True)
                ins.then_inc(gattn, 1)
            pe.wait_ge(mout_lo, 1)
            for c in range(3):
                t, r = c // 2, slice(c % 2 * GLA_CHUNK, (c % 2 + 1) * GLA_CHUNK)
                if c > 0:
                    pe.wait_ge(gturned, 2 * c)
                for h in range(GH):
                    ins = mm(bank[2 * c + h // 2][0:GDK, (h % 2) * GDV:(h % 2 + 1) * GDV],
                             ex[2][r, t, h * GDK:(h + 1) * GDK], z[r, t, A_V + h * GDV:A_V + (h + 1) * GDV],
                             start=True, stop=True)
                ins.then_inc(gkv, 1)
            for t in range(TB):
                pe.wait_ge(gattn_ready, t + 1)
                pe.wait_ge(gstate, 2 * t + 1)
                for h in range(GH):
                    o = bank[2 * t + h // 2][:, (h % 2) * GDV:(h % 2 + 1) * GDV]
                    ins = mm(o, attn[:, t, h, :], z[:, t, A_V + h * GDV:A_V + (h + 1) * GDV],
                             start=True, stop=False, skip_group_check=True)
                    for c in (1,) if t == 0 else (2, 3):
                        r = slice(c % 2 * GLA_CHUNK, (c % 2 + 1) * GLA_CHUNK)
                        ins = mm(o[r, :], qdT[:, t, h, r], state[c - 1][:, h, :], start=False, stop=True,
                                 skip_group_check=True)
                ins.then_inc(go, 1)

            def main_T(src):
                for b in range(3):
                    for k in (2 * b, 2 * b + 1):
                        for t in range(TB):
                            c = (k % 2) * TOK + t * P
                            ins = tr(bank[4 + b][:, c:c + P], src[:, t, k * P:(k + 1) * P], ident[:])
                    ins.then_inc(mainT, 1)

            pe.wait_ge(onorm, 2)
            main_T(z)
            project_out(U_OUT0, 0)

            pe.wait_ge(y_act, 2)
            pe.wait_ge(y_dve, 2)
            pe.wait_ge(normed, 3)
            to_T(xn, 3, lambda b: None)

            def gate_up(n, par, m):
                for i in range(2):
                    u = unit(n + i, KT, F_STEP, m)
                    for f in range(2):
                        for k in range(KT):
                            ins = passes(bank[2 * par + i][:, f * TOK:(f + 1) * TOK],
                                         [a[:, k, f * P:(f + 1) * P] for a in u], [a[:, k, :] for a in hT],
                                         k == 0, k == KT - 1)
                    ins.then_inc(weights_used, 1)

            def ffn_down(n, par, m, last=False):
                rows_product(unit(n, 2, D, m), 0, f_aT[par], 4, last).then_inc(weights_used, 1)

            pe.wait_ge(turned_lo, 16)
            seed(4)
            gate_up(U_FFN, 0, 0)
            with pe.Fori(0, (F_STEPS - 1) // 2) as i:
                for s in range(2):
                    j0 = s + 1
                    pe.wait_ge(f_act_ready, i * 2 + j0)
                    gate_up(U_FFN + 2 + 3 * s, j0 % 2, i)
                    pe.wait_ge(f_lo, i * 2 + (s + 1))
                    ffn_down(U_FFN + 4 + 3 * s, (j0 - 1) % 2, i)
            pe.wait_ge(f_lo, F_STEPS)
            ffn_down(U_B0 - 1, 0, 0, True)

            pe.wait_ge(y_act, 4)
            pe.wait_ge(y_dve, 4)
            pe.wait_ge(normed, 4)
            to_T(xn, 4, lambda b: None)
            pe.wait_ge(turned_lo, 20)
            chunk(U_B0, 512, (0, 1))
            chunk(U_B1, 512, (2, 3))
            pe.wait_ge(proj_act, 7)
            pe.wait_ge(proj_dve, 7)
            project(U_BV, 0, KT, SKV * HD, hT, (0, 1), True, True).then_inc(weights_used, 1)
            pe.wait_ge(proj_act, 8)
            pe.wait_ge(proj_dve, 8)
            mem_query(U_BQM, (2, 3))

            def free_b():
                pe.wait_ge(proj_act, 10)
                pe.wait_ge(proj_dve, 10)

            mem_attention(1, free_b)
            pe.wait_ge(roped, 1)
            for b in range(4):
                for i in range(2):
                    j = 2 * b + i
                    for t in range(TB):
                        src = qk[:, t, 2 * j:2 * j + 2, :].rearrange("p h d -> p (h d)")
                        ins = tr(bank[2 + b][:, i * TOK + t * P:i * TOK + (t + 1) * P], src, ident[:])
                ins.then_inc(sturn, 1)
            pe.wait_ge(sturned_a, 2)
            pe.wait_ge(sturned_d, 2)
            pe.wait_ge(mout_lo, 2)
            for j in range(6):
                if j >= 2:
                    pe.wait_ge(sscaled, 2 * (j - 1))
                for par in range(2):
                    r = slice(par * HD, (par + 1) * HD)
                    q, k = qkT[r, j, :], qkT[r, 6 + j // 3, :]
                    b = bank[(6, 7, 0, 1)[2 * (j % 2) + par]]
                    mm(b[:, 0:P], q[:, 0:P], k[:, 0:P], start=True, stop=True)
                    ins = mm(b[:, P:3 * P], q[:, P:TOK], k[:, 0:TOK], start=True, stop=True)
                    ins.then_inc(sscore, 1)
            pe.wait_ge(snorm, 2)
            for h in range(SH + 1):
                if h < SH:
                    if h >= 2:
                        pe.wait_ge(spturned_a if h % 2 == 0 else spturned_d, h // 2)
                    for i in range(3):
                        ins = tr(bank[2 + h % 2][:, i * P:(i + 1) * P], S[:, h, i * P:(i + 1) * P], ident[:])
                    ins.then_inc(spturn, 1)
                if h > 0:
                    g = h - 1
                    pe.wait_ge(spturned_a if g % 2 == 0 else spturned_d, g // 2 + 1)
                    kv = slice(g // 3 * HD, (g // 3 + 1) * HD)
                    o = bank[4 + g // 4][(g % 2) * HD:(g % 2 + 1) * HD, :]
                    c = g // 2 % 2 * TOK
                    mm(o[:, c:c + P], v_sb[:, 0, kv], spT[g % 4][:, 0:P], start=True, stop=True)
                    mm(o[:, c + P:c + TOK], v_sb[:, 0, kv], spT[g % 4][:, P:2 * P], start=True, stop=False)
                    ins = mm(o[:, c + P:c + TOK], v_sb[:, 1, kv], spT[g % 4][:, 2 * P:3 * P], start=False, stop=True)
                    ins.then_inc(sout, 1)
            project_out(U_OUT1, 1)

            pe.wait_ge(y_act, 6)
            pe.wait_ge(y_dve, 6)
            pe.wait_ge(normed, 5)
            to_T(xn, 5, lambda b: None)
            pe.wait_ge(turned_lo, 24)
            pe.wait_ge(router_lo, 1)
            for t in range(TB):
                for k in range(KT):
                    ins = passes(bank[t][:, 0:NE], [a[:, k, t * P:(t + 1) * P] for a in hT],
                                 [a[:, k, :] for a in router], k == 0, k == KT - 1)
            ins.then_inc(logits, 1)
            pe.wait_ge(mask_ready, 1)
            mask = [route[:, 64 + NE * t:64 + NE * (t + 1)] for t in range(TB)]
            mm(bank[2][:, 0:NE], before[:], mask[0], start=True, stop=True)
            mm(bank[3][:, 0:NE], ones[:], mask[0], start=True, stop=False)
            mm(bank[3][:, 0:NE], before[:], mask[1], start=False, stop=True)
            mm(bank[4][:, 0:NE], ones[:], mask[0], start=True, stop=False)
            mm(bank[4][:, 0:NE], ones[:], mask[1], start=False, stop=True).then_inc(ranks, 1)

            def expert_gate_up(i, n, m):
                for h in range(2):
                    u = unit(n + 2 * i + h, 4, E_STEP, m)
                    for k in range(4):
                        ins = passes(bank[i][:], [a[:, 4 * h + k, 0:P] for a in hT], [a[:, k, :] for a in u],
                                     h == 0 and k == 0, h == 1 and k == 3)
                    ins.then_inc(weights_used, 1)

            def expert_turn():
                for i in range(4):
                    ins = tr(bank[2][:, i * P:(i + 1) * P], e_act[:, i * P:(i + 1) * P], ident[:])
                ins.then_inc(e_turned, 1)

            def expert_down(n, m, first, last):
                for i in range(2):
                    u = unit(n + i, 2, D, m)
                    for k in range(2):
                        for h in range(2):
                            ins = passes(bank[3 + h][:], [a[:, 2 * i + k, :] for a in e_aT],
                                         [a[:, k, h * 512:(h + 1) * 512] for a in u],
                                         first and i == 0 and k == 0, last and i == 1 and k == 1)
                    ins.then_inc(weights_used, 1)

            def gather(count):
                pe.wait_ge(pick_made, count)
                for k in range(KT):
                    for b in range(TB):
                        ins = mm(bank[6 + k // 4][:, k % 4 * P:(k % 4 + 1) * P], xn[:, b, k * P:(k + 1) * P],
                                 pick[:, b, :], start=(b == 0), stop=(b == 1))
                    if k % 4 == 3:
                        ins.then_inc(gathered, 1)

            def first_gate(count, n, m):
                pe.wait_ge(gath_lo, count * 2)
                expert_gate_up(0, n, m)

            def middle_step(s, m, first):
                pe.wait_ge(e_silu_ready, s)
                expert_gate_up(0, U_EXP + 4, m)
                pe.wait_ge(e_act_ready, s)
                expert_turn()
                expert_gate_up(1, U_EXP + 4, m)
                pe.wait_ge(e_lo, s)
                expert_down(U_EXP + 8, m, first, False)

            gather(1)
            first_gate(1, U_EXP, 0)
            pe.wait_ge(routed, 1)
            rounds = pe.value_load(rounds_i[0:1, 0:1], min_val=1, max_val=ROUNDS)
            total = pe.snap(rounds * NE)
            with pe.Fori(0, total) as t:
                steps = pe.snap(t * E_STEPS)
                expert_gate_up(1, U_EXP, steps)
                pe.wait_ge(x_added, t * 4 + 1)
                for b in range(TB):
                    ins = tr(bank[2][:, b * P:(b + 1) * P], pick[:, b, :], ident[:])
                ins.then_inc(pick_turned, 1)
                pe.wait_ge(pickT_ready, t + 1)
                middle_step(pe.snap(steps + 1), steps, True)
                with pe.Fori(2, E_STEPS - 1) as j:
                    middle_step(pe.snap(steps + j), pe.snap(steps + (j - 1)), False)
                middle_step(pe.snap(steps + (E_STEPS - 1)), pe.snap(steps + (E_STEPS - 2)), False)
                pe.wait_ge(e_act_ready, steps + E_STEPS)
                expert_turn()
                with pe.If(total > t + 1):
                    gather(t + 2)
                pe.wait_ge(e_lo, steps + E_STEPS)
                expert_down(U_EXP + E_UNITS - 2, steps, False, True)
                with pe.If(total > t + 1):
                    first_gate(t + 2, U_EXP + E_UNITS, steps)
                for h in range(2):
                    pe.wait_ge(e_y_lo, t * 2 + (h + 1))
                    for b in range(TB):
                        o = bank[(6, 7, 5, 2)[2 * h + b]]
                        mm(o[:], pickT[:, b * P:(b + 1) * P], y_s[0][:, h * 512:(h + 1) * 512],
                           start=True, stop=False)
                        ins = mm(o[:], pickT[:, b * P:(b + 1) * P], y_s[1][:, h * 512:(h + 1) * 512],
                                 start=False, stop=True)
                        ins.then_inc(scattered, 1)

        @block.scalar
        def _(act):
            A = nc.scalar.activation
            fed = [0]

            def split(n, m=0, words=UNIT):
                act.wait_ge(weights_landed[n % RAW], m * 32 + 16 * (n // RAW + 1))
                if not isinstance(m, int) or n >= SPLIT:
                    act.wait_ge(weights_used, m * 6 + (n - SPLIT + 1))
                A(whi[n % SPLIT][:, 0:words], raw[n % RAW][:, 0:words], ACT.Copy).then_inc(weights_hi, 1)

            def feed(count):
                for _ in range(count):
                    split(fed[0], 0, size(fed[0]))
                    fed[0] += 1

            chain = [0]

            def then(ins):
                chain[0] += 1
                ins.then_inc(act_chain, 1)
                act.wait_ge(act_chain, chain[0])

            def root_mean_square(src, junk, col):
                for t in range(TB):
                    A(junk[:, t, :], src[:, t, :], ACT.Square,
                      accum_out=stats[:, col + t:col + t + 1]).then_inc(act_chain, 1)
                chain[0] += 2
                act.wait_ge(act_chain, chain[0])
                A(stats[:, col:col + 2], stats[:, col:col + 2], ACT.Sqrt, bias=EPS,
                  scale=1.0 / D).then_inc(root_ready, 1)

            def turned_hi_of(dst, call, gain_col):
                for b in range(4):
                    act.wait_ge(turned, 4 * call + b + 1)
                    for i in range(2):
                        k = 2 * b + i
                        ins = A(dst[:, k, :], bank[4 + b][:, i * TOK:(i + 1) * TOK], ACT.Copy,
                                scale=gains[:, gain_col + k:gain_col + k + 1])
                    ins.then_inc(turned_hi, 1)

            def chunk_out(dst, b, last_unit, s=proj_act):
                act.wait_ge(weights_used, last_unit + 1)
                A(dst, b, ACT.Copy).then_inc(s, 1)

            def qk_out(half, b, last_unit):
                act.wait_ge(weights_used, last_unit + 1)
                for dst, src in qk_pieces(0, half, b):
                    ins = A(dst, src, ACT.Copy)
                ins.then_inc(proj_act, 1)

            def mem_attention(l):
                for t in range(TB):
                    act.wait_ge(mmax, 2 * l + t + 1)
                    for par in range(2):
                        for i in range(2):
                            c = 4 * t + 2 * par + i
                            ins = A(mp[:, t, par, i, :], bank[1 + 2 * t + par][:, i * TOK:(i + 1) * TOK], ACT.Exp,
                                    bias=small[:, 8 + c:9 + c], scale=HD ** -0.5,
                                    accum_out=small[:, 16 + c:17 + c])
                            ins.then_inc(mprob, 1)
                for t in range(TB):
                    for par in range(2):
                        act.wait_ge(mturn, 4 * l + 2 * t + par + 1)
                        src = bank[(5, 6, 7, 0)[2 * t + par]][:].rearrange("p (i m s) -> p i m s", i=2, m=2)
                        for i in range(2):
                            ins = A(mpT[:, par, i, :, t * P:(t + 1) * P], src[:, i], ACT.Copy)
                        ins.then_inc(mturned, 1)
                act.wait_ge(mout, l + 1)
                A(mT[0][:, 6:8, :].rearrange("p a b -> p (a b)"), bank[1][:], ACT.Copy).then_inc(mout_hi, 1)

            def main_hi(b, waits):
                waits()
                A(mT[0][:, 2 * b:2 * b + 2, :].rearrange("p a b -> p (a b)"), bank[4 + b][:],
                  ACT.Copy).then_inc(mainT_hi, 1)

            def y_out(b0, last_unit):
                act.wait_ge(weights_used, last_unit + 1)
                for h in range(2):
                    A(x[:, 0, h * 512:(h + 1) * 512], bank[b0 + h][:], ACT.Copy).then_inc(y_act, 1)

            act.wait_ge(consts, 1)
            act.wait_ge(mem_loaded, 16)
            root_mean_square(memn, xn, 0)
            feed(1)
            act.wait_ge(x_loaded, 16)
            root_mean_square(x, xn, 2)
            feed(5)
            act.wait_ge(gains_ready, 1)
            turned_hi_of(mT[0], 0, 16)
            feed(2)
            act.wait_ge(weights_used, U_KV0 + 2)
            for i in range(2):
                ins = A(kmT[0][:, i, :], bank[i][:, 0:TOK], ACT.Copy)
            ins.then_inc(kv_act, 1)
            turned_hi_of(hT[0], 1, 0)
            feed(2)
            chunk_out(z[:, 0, 1536:2048], bank[0][:], U_A0 + 1)
            turned_hi_of(mT[0], 2, 24)
            feed(2)
            chunk_out(z[:, 0, 0:512], bank[2][:], U_A1 + 1)
            feed(2)
            act.wait_ge(weights_used, U_KV1 + 2)
            for i in range(2):
                ins = A(kmT[1][:, i, :], bank[4 + i][:, 0:TOK], ACT.Copy)
            ins.then_inc(kv_act, 1)
            feed(2)
            chunk_out(z[:, 0, 512:1024], bank[0][:], U_A2 + 1)
            feed(1)
            for t in range(TB):
                act.wait_ge(gate_logits, t + 1)
                then(A(abs_g[:, t, :], bank[5 + t][:, 0:GQK], ACT.Abs))
                then(A(abs_g[:, t, :], abs_g[:, t, :], ACT.Exp, scale=-1.0))
                A(ln_g[:, t, :], abs_g[:, t, :], ACT.Ln, bias=1.0).then_inc(ln_ready, 1)
            feed(1)
            chunk_out(z[:, 0, 1024:1536], bank[2][:], U_A3 + 1)
            feed(1)
            for t in range(TB):
                act.wait_ge(cum_done, t + 1)
                cum, rem = bank[(4, 5)[t]][:, 0:GQK], bank[(7, 6)[t]][:, 0:GQK]
                A(ex[0][:, t, :], cum, ACT.Exp).then_inc(gexp, 1)
                A(ex[1][:, t, :], cum, ACT.Exp, scale=-1.0).then_inc(gexp, 1)
                A(ex[2][:, t, :], rem, ACT.Exp).then_inc(gexp, 1)
            feed(1)
            chunk_out(z[:, 0, 2048:A_QM], bank[0][:, 0:A_QM - 2048], U_A4 + 1)
            feed(1)
            chunk_out(qmT[:, 0, :], bank[2][:, 0:TOK], U_AQM)
            act.wait_ge(decay_done, 1)
            for i in range(2):
                A(small[0:GDK, 32 + 4 * i:36 + 4 * i], bank[i][0:GDK, 0:GH], ACT.Exp).then_inc(decay_ready, 1)
            mem_attention(0)
            act.wait_ge(proj_act, 5)
            act.wait_ge(proj_dve, 5)
            for t in range(TB):
                A(z[:, t, A_R:A_QM], z[:, t, A_R:A_QM], ACT.Silu).then_inc(silu_r, 1)
            for i in range(4):
                act.wait_ge(gturn, i + 1)
                dst = (qdT, kdT)[i % 2]
                A(dst[:, i // 2].rearrange("p h s -> p (h s)"), bank[2 + i][0:GDK, :], ACT.Copy).then_inc(gturned, 1)
            for t in range(TB):
                act.wait_ge(go, t + 1)
                for b in range(2):
                    for h in range(2):
                        c = 40 + 4 * t + 2 * b + h
                        A(squares[:, 2 * b + h, :], bank[2 * t + b][:, h * GDV:(h + 1) * GDV], ACT.Square,
                          accum_out=small[:, c:c + 1]).then_inc(act_chain, 1)
                chain[0] += GH
                act.wait_ge(act_chain, chain[0])
                A(small[:, 40 + 4 * t:44 + 4 * t], small[:, 40 + 4 * t:44 + 4 * t], ACT.Sqrt, bias=EPS,
                  scale=1.0 / GDV).then_inc(oroot, 1)
            for b in range(3):
                main_hi(b, lambda: act.wait_ge(mainT, b + 1))
            feed(4)
            y_out(0, U_OUT0 + 3)
            act.wait_ge(y_act, 2)
            act.wait_ge(y_dve, 2)
            root_mean_square(x, xn, 4)
            turned_hi_of(hT[0], 3, 32)

            def ffn_silu(par, last_unit, m, done):
                act.wait_ge(weights_used, m * 6 + (last_unit + 1))
                if done is not None:
                    act.wait_ge(f_act_ready, done)
                A(f_silu[par][:], bank[2 * par][:], ACT.Silu).then_inc(f_silu_ready, 1)

            def ffn_hi(par, steps_done):
                act.wait_ge(f_act_ready, steps_done + 1)
                A(f_aT[par][0][:].rearrange("p a b -> p (a b)"), f_act[par][:], ACT.Copy).then_inc(f_hi, 1)

            assert fed[0] == U_FFN + SPLIT, fed
            feed(2)
            ffn_silu(0, U_FFN, 0, None)
            ffn_hi(0, 1)
            n0 = fed[0]
            with act.Fori(0, (F_STEPS - 1) // 2) as i:
                for s in range(2):
                    par = (s + 1) % 2
                    split(n0 + 3 * s, i)
                    split(n0 + 3 * s + 1, i)
                    ffn_silu(par, U_FFN + 2 + 3 * s, i, i * 2 + (s + 1))
                    ffn_hi(par, i * 2 + (s + 2))
                    split(n0 + 3 * s + 2, i)
            fed[0] = n0 + 30
            assert fed[0] == U_B0 - 1 + SPLIT
            feed(1)
            y_out(4, U_B0 - 1)

            act.wait_ge(y_act, 4)
            act.wait_ge(y_dve, 4)
            root_mean_square(x, xn, 6)
            turned_hi_of(hT[0], 4, 8)
            act.wait_ge(angles, 1)
            A(rope_c[:, 1], rope_c[:, 0], ACT.Sin).then_inc(sincos, 1)
            A(rope_c[:, 2], rope_c[:, 2], ACT.Sin).then_inc(sincos, 1)
            feed(2)
            qk_out(0, bank[0], U_B0 + 1)
            feed(2)
            qk_out(1, bank[2], U_B1 + 1)
            feed(U_EXP - fed[0])
            chunk_out(v_sb[:, 0, :], bank[0][:, 0:MEM_W], U_BV)
            chunk_out(qmT[:, 0, :], bank[2][:, 0:TOK], U_BQM)
            mem_attention(1)
            for b in (0, 2):
                act.wait_ge(sturn, b + 1)
                A(qkT[:, 2 * b:2 * b + 2, :].rearrange("p a b -> p (a b)"), bank[2 + b][:],
                  ACT.Copy).then_inc(sturned_a, 1)
            act.wait_ge(smax, 1)
            for t in range(TB):
                for h in range(SH):
                    s = S[:, h, 0:P] if t == 0 else S[:, h, P:3 * P]
                    A(s, s, ACT.Exp, bias=swa[:, 1, t * SH + h:t * SH + h + 1],
                      accum_out=swa[:, 2, t * SH + h:t * SH + h + 1]).then_inc(sprob, 1)
                if t == 0:
                    act.wait_ge(ssink, 1)
                    A(swa[:, 3, :], swa[:, 3, :], ACT.Exp).then_inc(ssink, 1)
            for h in range(0, SH, 2):
                act.wait_ge(spturn, h + 1)
                if h >= 4:
                    act.wait_ge(sout, h - 3)
                A(spT[h % 4][:], bank[2][:, 0:3 * P], ACT.Copy).then_inc(spturned_a, 1)
                if h in (4, 8):
                    b = h // 4 - 1
                    main_hi(b, lambda: act.wait_ge(sout, 4 * b + 4))
            main_hi(2, lambda: act.wait_ge(sout, SH))
            y_out(0, U_OUT1 + 3)
            act.dma_start(final_gain[:], final_norm.partition_broadcast(P)).then_inc(final_gain_loaded, 16)

            act.wait_ge(y_act, 6)
            act.wait_ge(y_dve, 6)
            root_mean_square(x, xn, 8)
            feed(2)
            turned_hi_of(hT[0], 5, 40)
            act.wait_ge(params_loaded, 16 * 9)
            A(router[0][:].rearrange("p k e -> p (k e)"), router_raw[:].rearrange("p k e -> p (k e)"),
              ACT.Copy).then_inc(router_hi, 1)
            feed(2)
            act.wait_ge(gap_ready, 1)
            A(route[:, 32:34], route[:, 32:34], ACT.Exp).then_inc(gap_exp, 1)
            feed(2)
            assert fed[0] == U_EXP + SPLIT

            def gathered_hi(count):
                for b in range(2):
                    act.wait_ge(gathered, count * 2 + (b - 1))
                    for k in range(4):
                        ins = A(hT[0][:, 4 * b + k, 0:P], bank[6 + b][:, k * P:(k + 1) * P], ACT.Copy,
                                scale=gains[:, 40 + 4 * b + k:41 + 4 * b + k])
                    ins.then_inc(gath_hi, 1)

            def down_hi(s):
                act.wait_ge(e_turned, s)
                A(e_aT[0], bank[2][:].rearrange("p (a b) -> p a b", a=4), ACT.Copy).then_inc(e_hi, 1)

            def middle_step(m, s, splits):
                for i in range(2):
                    split(U_EXP + 10 + i, m)
                down_hi(s)
                act.wait_ge(weights_used, m * 6 + (U_EXP + 6))
                act.wait_ge(e_act_ready, s)
                A(e_silu[:], bank[0][:], ACT.Silu).then_inc(e_silu_ready, 1)
                for i in range(2, splits):
                    split(U_EXP + 10 + i, m)

            gathered_hi(1)
            act.wait_ge(routed, 1)
            rounds = act.value_load(rounds_i[0:1, 0:1], min_val=1, max_val=ROUNDS)
            total = act.snap(rounds * NE)
            with act.Fori(0, total) as t:
                steps = act.snap(t * E_STEPS)
                for i in range(2):
                    split(U_EXP + SPLIT + i, steps)
                A(e_silu[:], bank[0][:], ACT.Silu).then_inc(e_silu_ready, 1)
                act.wait_ge(pick_turned, t + 1)
                A(pickT[:], bank[2][:, 0:TOK], ACT.Copy).then_inc(pickT_ready, 1)
                for i in range(2, 4):
                    split(U_EXP + SPLIT + i, steps)
                with act.Fori(1, E_STEPS - 1) as j:
                    middle_step(act.snap(steps + (j - 1)), act.snap(steps + j), 6)
                middle_step(act.snap(steps + (E_STEPS - 2)), act.snap(steps + (E_STEPS - 1)), 2)
                with act.If(total > t + 1):
                    split(U_EXP + E_UNITS, steps)
                    split(U_EXP + E_UNITS + 1, steps)
                down_hi(steps + E_STEPS)
                with act.If(total > t + 1):
                    split(U_EXP + E_UNITS + 2, steps)
                    gathered_hi(t + 2)
                    split(U_EXP + E_UNITS + 3, steps)
                act.wait_ge(weights_used, steps * 6 + (U_EXP + E_UNITS))
                for h in range(2):
                    A(y_s[0][:, h * 512:(h + 1) * 512], bank[3 + h][:], ACT.Copy).then_inc(e_y_hi, 1)
                with act.If(total > t + 1):
                    split(U_EXP + E_UNITS + 4, steps)
                    split(U_EXP + E_UNITS + 5, steps)

            act.wait_ge(x_added, rounds * (NE * 4) + 1)
            root_mean_square(x, xn, 10)

        @block.vector
        def _(dve):
            V = nc.vector
            MUL, ADD, SUB = ALU.mult, ALU.add, ALU.subtract
            fed = [0]

            def split(n, m=0, words=UNIT):
                dve.wait_ge(weights_hi, m * 6 + (n + 1))
                V.tensor_tensor(wlo[n % SPLIT][:, 0:words], raw[n % RAW][:, 0:words],
                                whi[n % SPLIT][:, 0:words].bitcast(F32), SUB).then_inc(weights_lo, 1)

            def feed(count):
                for _ in range(count):
                    split(fed[0], 0, size(fed[0]))
                    fed[0] += 1

            chain = [0]

            def then(ins):
                chain[0] += 1
                ins.then_inc(dve_chain, 1)
                dve.wait_ge(dve_chain, chain[0])

            def normalise(dst, src, col, count):
                dve.wait_ge(root_ready, count)
                then(V.reciprocal(stats[:, col:col + 2], stats[:, col:col + 2]))
                for t in range(TB):
                    ins = V.tensor_scalar(dst[:, t, :], src[:, t, :], stats[:, col + t:col + t + 1], None, MUL)
                ins.then_inc(normed, 1)

            def turned_lo_of(dst, call, gain_col):
                for b in range(4):
                    dve.wait_ge(turned_hi, 4 * call + b + 1)
                    for i in range(2):
                        k = 2 * b + i
                        ins = V.scalar_tensor_tensor(
                            dst[1][:, k, :], bank[4 + b][:, i * TOK:(i + 1) * TOK],
                            gains[:, gain_col + k:gain_col + k + 1], dst[0][:, k, :].bitcast(F32), MUL, SUB)
                    ins.then_inc(turned_lo, 1)

            def chunk_out(dst, b, last_unit):
                dve.wait_ge(weights_used, last_unit + 1)
                V.tensor_copy(dst, b).then_inc(proj_dve, 1)

            def qk_out(half, b, last_unit):
                dve.wait_ge(weights_used, last_unit + 1)
                for dst, src in qk_pieces(1, half, b):
                    ins = V.tensor_copy(dst, src)
                ins.then_inc(proj_dve, 1)

            def mem_attention(l):
                for t in range(TB):
                    dve.wait_ge(mscore, 2 * l + t + 1)
                    for par in range(2):
                        c = 4 * t + 2 * par
                        V.tensor_reduce(small[:, c:c + 2], bank[1 + 2 * t + par][:].rearrange("p (i s) -> p i s", i=2),
                                        AX.X, ALU.max).then_inc(dve_chain, 1)
                    chain[0] += 2
                    dve.wait_ge(dve_chain, chain[0])
                    V.tensor_scalar(small[:, 8 + 4 * t:12 + 4 * t], small[:, 4 * t:4 * t + 4], -HD ** -0.5, None,
                                    MUL).then_inc(mmax, 1)
                for t in range(TB):
                    dve.wait_ge(mprob, 8 * l + 4 * t + 4)
                    den = small[:, 16 + 4 * t:20 + 4 * t]
                    then(V.reciprocal(den, den))
                    probs = mp[:, t].rearrange("p r i s -> p (r i) s")
                    V.tensor_tensor(probs, probs, den.unsqueeze(2).broadcast_to([P, 4, TOK]), MUL).then_inc(mnorm, 1)

            def mem_out_lo(l):
                dve.wait_ge(mout_hi, l + 1)
                V.tensor_tensor(mT[1][:, 6:8, :].rearrange("p a b -> p (a b)"), bank[1][:],
                                mT[0][:, 6:8, :].bitcast(F32).rearrange("p a b -> p (a b)"), SUB).then_inc(mout_lo, 1)

            def main_lo(b, l):
                dve.wait_ge(mainT_hi, 3 * l + b + 1)
                V.tensor_tensor(mT[1][:, 2 * b:2 * b + 2, :].rearrange("p a b -> p (a b)"), bank[4 + b][:],
                                mT[0][:, 2 * b:2 * b + 2, :].bitcast(F32).rearrange("p a b -> p (a b)"),
                                SUB).then_inc(mainT_lo, 1)

            def y_out(b0, last_unit):
                dve.wait_ge(weights_used, last_unit + 1)
                for h in range(2):
                    V.tensor_copy(x[:, 1, h * 512:(h + 1) * 512], bank[b0 + 2 + h][:]).then_inc(y_dve, 1)

            dve.wait_ge(gains_turned, 1)
            V.tensor_copy(gains[:], bank[0][:, 0:48]).then_inc(gains_ready, 1)
            normalise(memn, memn, 0, 1)
            feed(1)
            dve.wait_ge(x_loaded, 16)
            normalise(xn, x, 2, 2)
            feed(5)
            turned_lo_of(mT, 0, 16)
            feed(2)
            dve.wait_ge(weights_used, U_KV0 + 2)
            for t in range(TB):
                ins = V.tensor_copy(vm[0][:, t, :], bank[2 + t][:, 0:MEM_W])
            ins.then_inc(kv_dve, 1)
            turned_lo_of(hT, 1, 0)
            feed(2)
            chunk_out(z[:, 1, 1536:2048], bank[1][:], U_A0 + 1)
            turned_lo_of(mT, 2, 24)
            feed(2)
            chunk_out(z[:, 1, 0:512], bank[3][:], U_A1 + 1)
            feed(2)
            dve.wait_ge(weights_used, U_KV1 + 2)
            for t in range(TB):
                ins = V.tensor_copy(vm[1][:, t, :], bank[6 + t][:, 0:MEM_W])
            ins.then_inc(kv_dve, 1)
            then(V.memset(glrT[:], 1.0))
            feed(2)
            chunk_out(z[:, 1, 512:1024], bank[1][:], U_A2 + 1)
            dve.wait_ge(glr_turned, 1)
            V.tensor_copy(glrT[0:LOWRANK, :], bank[4][0:LOWRANK, 0:TOK]).then_inc(glr_ready, 1)
            feed(1)
            for t in range(TB):
                dve.wait_ge(ln_ready, t + 1)
                V.scalar_tensor_tensor(la[:, t, :], bank[5 + t][:, 0:GQK], 0.0, ln_g[:, t, :],
                                       ALU.min, SUB).then_inc(la_ready, 1)
            feed(1)
            chunk_out(z[:, 1, 1024:1536], bank[3][:], U_A3 + 1)
            feed(1)
            dve.wait_ge(proj_act, 3)
            dve.wait_ge(proj_dve, 3)
            for t in range(TB):
                q, k = z[:, t, 0:GQK], z[:, t, GQK:2 * GQK]
                dve.wait_ge(gexp, 3 * t + 3)
                V.scalar_tensor_tensor(q, q, GDK ** -0.5, ex[0][:, t, :], MUL, MUL).then_inc(gdec, 1)
                V.tensor_tensor(ex[2][:, t, :], k, ex[2][:, t, :], MUL).then_inc(gdec, 1)
                V.tensor_tensor(k, k, ex[1][:, t, :], MUL).then_inc(gdec, 1)
            feed(1)
            chunk_out(z[:, 1, 2048:A_QM], bank[1][:, 0:A_QM - 2048], U_A4 + 1)
            feed(1)
            chunk_out(qmT[:, 1, :], bank[3][:, 0:TOK], U_AQM)
            mem_attention(0)
            mem_out_lo(0)
            for t in range(TB):
                dve.wait_ge(gattn, t + 1)
                V.tensor_tensor(attn[:, t], bank[6 + t][:].rearrange("p (h s) -> p h s", h=GH),
                                causal[:].unsqueeze(1).broadcast_to([P, GH, P]), MUL).then_inc(gattn_ready, 1)
            dve.wait_ge(decay_ready, 2)
            for c in range(3):
                dve.wait_ge(gkv, c + 1)
                if c == 0:
                    for b in range(2):
                        ins = V.tensor_copy(state[0][:, 2 * b:2 * b + 2, :],
                                            bank[b][0:GDK, 0:2 * GDV].rearrange("p (h v) -> p h v", h=2))
                else:
                    dve.wait_ge(gstate, c)
                    for h in range(GH):
                        d = 32 + 4 * (c - 1) + h
                        ins = V.scalar_tensor_tensor(
                            state[c][:, h, :], state[c - 1][:, h, :], small[0:GDK, d:d + 1],
                            bank[2 * c + h // 2][0:GDK, (h % 2) * GDV:(h % 2 + 1) * GDV], MUL, ADD)
                ins.then_inc(gstate, 1)
            for t in range(TB):
                dve.wait_ge(silu_r, t + 1)
                r = z[:, t, A_R:A_QM].rearrange("p (h v) -> p h v", h=GH)
                ins = V.tensor_tensor(r, r, gla_gain[:].unsqueeze(1).broadcast_to([P, GH, GDV]), MUL)
                then(ins)
            for t in range(TB):
                dve.wait_ge(oroot, t + 1)
                c = 40 + 4 * t
                then(V.reciprocal(small[:, c:c + 4], small[:, c:c + 4]))
                for h in range(GH):
                    o = bank[2 * t + h // 2][:, h % 2 * GDV:(h % 2 + 1) * GDV]
                    ins = V.scalar_tensor_tensor(o_sb[:, t, h, :], o, small[:, c + h:c + h + 1],
                                                 z[:, t, A_R + h * GDV:A_R + (h + 1) * GDV], MUL, MUL)
                ins.then_inc(onorm, 1)
            for b in range(3):
                main_lo(b, 0)
            feed(4)
            y_out(0, U_OUT0 + 3)
            V.sem_inc(f_act_ready, 1)
            normalise(xn, x, 4, 3)
            turned_lo_of(hT, 3, 32)

            def ffn_act(par, up_unit, m, done):
                dve.wait_ge(weights_used, m * 6 + (up_unit + 1))
                dve.wait_ge(f_silu_ready, done)
                V.tensor_tensor(f_act[par][:], f_silu[par][:], bank[2 * par + 1][:], MUL).then_inc(f_act_ready, 1)
                dve.wait_ge(f_hi, done)
                V.tensor_tensor(f_aT[par][1][:].rearrange("p a b -> p (a b)"), f_act[par][:],
                                f_aT[par][0][:].bitcast(F32).rearrange("p a b -> p (a b)"), SUB).then_inc(f_lo, 1)

            assert fed[0] == U_FFN + SPLIT, fed
            feed(2)
            ffn_act(0, U_FFN + 1, 0, 1)
            n0 = fed[0]
            with dve.Fori(0, (F_STEPS - 1) // 2) as i:
                for s in range(2):
                    split(n0 + 3 * s, i)
                    split(n0 + 3 * s + 1, i)
                    ffn_act((s + 1) % 2, U_FFN + 3 + 3 * s, i, i * 2 + (s + 2))
                    split(n0 + 3 * s + 2, i)
            fed[0] = n0 + 30
            feed(1)
            y_out(4, U_B0 - 1)

            normalise(xn, x, 6, 4)
            turned_lo_of(hT, 4, 8)
            ang, turn = rope_c[:, 0], rope_c[:, 3]
            freq = ROPE_THETA ** (-np.arange(ROPE_HALF) / ROPE_HALF)
            dve.wait_ge(params_loaded, 16 * 9)
            then(V.tensor_copy(stats[:, 20:22], pos_i[:]))
            for i in range(ROPE_HALF):
                ins = V.tensor_scalar(ang.rearrange("p (t i) -> p t i", t=TB)[:, :, i:i + 1],
                                      stats[:, 20:22].unsqueeze(2), float(np.float32(freq[i])), None, MUL)
            then(ins)
            magic = 1.5 * 2 ** 23
            then(V.tensor_scalar(turn, ang, 1 / (2 * math.pi), magic, MUL, ADD))
            then(V.tensor_scalar(turn, turn, magic, None, SUB))
            c1 = 6.28125
            c2 = float(np.float32(round((2 * math.pi - c1) * 2 ** 17) / 2 ** 17))
            for c in (c1, c2, 2 * math.pi - c1 - c2):
                then(V.scalar_tensor_tensor(ang, turn, -c, ang, MUL, ADD))
            edge = float(np.nextafter(np.float32(math.pi), np.float32(0)))
            then(V.tensor_scalar(ang, ang, edge, -edge, ALU.min, ALU.max))
            then(V.scalar_tensor_tensor(rope_c[:, 2], ang, -1.0, ang, MUL, ALU.max))
            V.tensor_scalar(rope_c[:, 2], rope_c[:, 2], -1.0, math.pi / 2, MUL, ADD).then_inc(angles, 1)
            feed(2)
            qk_out(0, bank[1], U_B0 + 1)
            feed(2)
            qk_out(1, bank[3], U_B1 + 1)
            dve.wait_ge(sincos, 2)
            dve.wait_ge(proj_act, 8)
            dve.wait_ge(proj_dve, 8)
            for t in range(TB):
                def per_head(a):
                    return a[:, t * 8:t * 8 + 8].unsqueeze(1).broadcast_to([P, SH + SKV, ROPE_HALF])

                sin, cos = per_head(rope_c[:, 1]), per_head(rope_c[:, 2])
                x1, x2 = qk[:, t, :, 0:ROPE_HALF], qk[:, t, :, ROPE_HALF:2 * ROPE_HALF]
                for i, (a, b) in enumerate(((x1, cos), (x2, sin), (x2, cos), (x1, sin))):
                    ins = V.tensor_tensor(rope[i][:, t], a, b, MUL)
                then(ins)
                V.tensor_tensor(x1, rope[0][:, t], rope[1][:, t], SUB)
                ins = V.tensor_tensor(x2, rope[2][:, t], rope[3][:, t], ADD)
            ins.then_inc(roped, 1)
            chunk_out(v_sb[:, 1, :], bank[1][:, 0:MEM_W], U_BV)
            chunk_out(qmT[:, 1, :], bank[3][:, 0:TOK], U_BQM)
            mem_attention(1)
            mem_out_lo(1)
            for b in (1, 3):
                dve.wait_ge(sturn, b + 1)
                V.tensor_copy(qkT[:, 2 * b:2 * b + 2, :].rearrange("p a b -> p (a b)"),
                              bank[2 + b][:]).then_inc(sturned_d, 1)
            for j in range(6):
                for par in range(2):
                    dve.wait_ge(sscore, 2 * j + par + 1)
                    V.scalar_tensor_tensor(S[:, Q_PAIRS[j][par], :], bank[(6, 7, 0, 1)[2 * (j % 2) + par]][:, 0:3 * P],
                                           HD ** -0.5, window[:], MUL, ADD).then_inc(sscaled, 1)
            dve.wait_ge(sscaled, SH)
            for t in range(TB):
                s = S[:, :, 0:P] if t == 0 else S[:, :, P:3 * P]
                m = swa[:, 0, t * SH:(t + 1) * SH]
                then(V.tensor_reduce(m, s, AX.X, ALU.max))
                then(V.tensor_tensor(m, m, sinks[:], ALU.max))
            V.tensor_scalar(swa[:, 1, :], swa[:, 0, :], -1.0, None, MUL).then_inc(smax, 1)
            for t in range(TB):
                ins = V.tensor_tensor(swa[:, 3, t * SH:(t + 1) * SH], sinks[:], swa[:, 0, t * SH:(t + 1) * SH], SUB)
            ins.then_inc(ssink, 1)
            dve.wait_ge(ssink, 2)
            for t in range(TB):
                dve.wait_ge(sprob, SH * (t + 1))
                den = swa[:, 2, t * SH:(t + 1) * SH]
                then(V.tensor_tensor(den, den, swa[:, 3, t * SH:(t + 1) * SH], ADD))
                then(V.reciprocal(den, den))
                s = S[:, :, 0:P] if t == 0 else S[:, :, P:3 * P]
                V.tensor_tensor(s, s, den.unsqueeze(2).broadcast_to([P, SH, P * (t + 1)]), MUL).then_inc(snorm, 1)
            for h in range(1, SH, 2):
                dve.wait_ge(spturn, h + 1)
                if h >= 4:
                    dve.wait_ge(sout, h - 3)
                V.tensor_copy(spT[h % 4][:], bank[3][:, 0:3 * P]).then_inc(spturned_d, 1)
                if h in (5, 9):
                    main_lo(h // 4 - 1, 1)
            main_lo(2, 1)
            y_out(0, U_OUT1 + 3)

            normalise(xn, x, 8, 5)
            feed(2)
            turned_lo_of(hT, 5, 40)
            dve.wait_ge(router_hi, 1)
            V.tensor_tensor(router[1][:].rearrange("p k e -> p (k e)"), router_raw[:].rearrange("p k e -> p (k e)"),
                            router[0][:].bitcast(F32).rearrange("p k e -> p (k e)"), SUB).then_inc(router_lo, 1)
            feed(2)
            dve.wait_ge(logits, 1)
            for t in range(TB):
                ins = V.tensor_copy(route[:, NE * t:NE * (t + 1)], bank[t][:, 0:NE])
            then(ins)
            for t in range(TB):
                ins = V.max(route[:, 16 + 8 * t:24 + 8 * t], route[:, NE * t:NE * (t + 1)])
            then(ins)
            for t in range(TB):
                ins = V.max_index(route_u[:, t, :], route[:, 16 + 8 * t:24 + 8 * t], route[:, NE * t:NE * (t + 1)])
            top = route[:, 16:32].rearrange("p (t i) -> p t i", t=TB)
            then(ins)
            V.tensor_tensor(route[:, 32:34].unsqueeze(2), top[:, :, 1:2], top[:, :, 0:1], SUB).then_inc(gap_ready, 1)
            for t in range(TB):
                ins = V.tensor_copy(route[:, 40 + 2 * t:42 + 2 * t], route_u[:, t, 0:2])
            then(ins)
            for t in range(TB):
                for i in range(2):
                    c = 160 + 16 * t + 8 * i
                    ins = V.tensor_scalar(route[:, c:c + 8], iota[:, 0:NE], route[:, 40 + 2 * t + i:41 + 2 * t + i],
                                          None, ALU.is_equal)
            then(ins)
            for t in range(TB):
                c = 160 + 16 * t
                ins = V.tensor_tensor(route[:, 64 + NE * t:72 + NE * t], route[:, c:c + 8], route[:, c + 8:c + 16], ADD)
            ins.then_inc(mask_ready, 1)
            dve.wait_ge(gap_exp, 1)
            then(V.tensor_scalar(route[:, 34:36], route[:, 32:34], 1.0, None, ADD))
            then(V.reciprocal(route[:, 34:36], route[:, 34:36]))
            then(V.tensor_tensor(route[:, 36:38], route[:, 34:36], route[:, 32:34], MUL))
            for t in range(TB):
                c = 160 + 16 * t
                ins = V.tensor_scalar(route[:, c:c + 8], route[:, c:c + 8], route[:, 34 + t:35 + t], None, MUL)
            then(ins)
            for t in range(TB):
                c = 160 + 16 * t
                for r in range(ROUNDS):
                    g = 128 + 16 * t + NE * r
                    ins = V.scalar_tensor_tensor(route[:, g:g + 8], route[:, c + 8:c + 16], route[:, 36 + t:37 + t],
                                                 route[:, c:c + 8], MUL, ADD)
            then(ins)
            dve.wait_ge(ranks, 1)
            for t in range(TB):
                for r in range(ROUNDS):
                    c = 96 + 16 * t + NE * r
                    ins = V.scalar_tensor_tensor(route[:, c:c + 8], bank[2 + t][:, 0:NE], 1.0 - P * r,
                                                 route[:, 64 + NE * t:72 + NE * t], ADD, MUL)
            then(ins)
            then(V.tensor_scalar(route[:, 96:128], route[:, 96:128], 1.0, None, SUB))
            then(V.tensor_reduce(route[0:1, 38:39], bank[4][0:1, 0:NE], AX.X, ALU.max))
            V.tensor_scalar(rounds_i[:], route[0:1, 38:39], float(P), 1.0, ALU.is_gt, ADD).then_inc(routed, 1)

            def make_pick(t):
                for b in range(TB):
                    c = t + (96 + 16 * b)
                    slot = route[:, c:c + 1] if isinstance(t, int) else route[:, bass.ds(c, 1)]
                    ins = V.tensor_scalar(pick[:, b, :], iota[:], slot, None, ALU.is_equal)
                ins.then_inc(pick_made, 1)

            def gathered_lo(count):
                for b in range(2):
                    dve.wait_ge(gath_hi, count * 2 + (b - 1))
                    for k in range(4):
                        ins = V.scalar_tensor_tensor(
                            hT[1][:, 4 * b + k, 0:P], bank[6 + b][:, k * P:(k + 1) * P],
                            gains[:, 40 + 4 * b + k:41 + 4 * b + k], hT[0][:, 4 * b + k, 0:P].bitcast(F32),
                            MUL, SUB)
                    ins.then_inc(gath_lo, 1)

            def activate(s, up_unit, m):
                dve.wait_ge(weights_used, m * 6 + (up_unit + 1))
                dve.wait_ge(e_silu_ready, s)
                V.tensor_tensor(e_act[:], e_silu[:], bank[1][:], MUL).then_inc(e_act_ready, 1)

            def down_lo(s):
                dve.wait_ge(e_hi, s)
                V.tensor_tensor(e_aT[1], bank[2][:].rearrange("p (a b) -> p a b", a=4),
                                e_aT[0].bitcast(F32), SUB).then_inc(e_lo, 1)

            V.sem_inc(x_added, 1)
            dve.wait_ge(routed, 1)
            make_pick(0)
            feed(2)
            assert fed[0] == U_EXP + SPLIT
            gathered_lo(1)
            rounds = dve.value_load(rounds_i[0:1, 0:1], min_val=1, max_val=ROUNDS)
            total = dve.snap(rounds * NE)
            with dve.Fori(0, total) as t:
                steps = dve.snap(t * E_STEPS)
                for i in range(2):
                    split(U_EXP + SPLIT + i, steps)
                activate(steps + 1, U_EXP + 3, steps)
                for i in range(2, 4):
                    split(U_EXP + SPLIT + i, steps)
                with dve.Fori(1, E_STEPS - 1) as j:
                    m, s = dve.snap(steps + (j - 1)), dve.snap(steps + j)
                    for i in range(2):
                        split(U_EXP + 10 + i, m)
                    down_lo(s)
                    for i in range(2, 4):
                        split(U_EXP + 10 + i, m)
                    activate(s + 1, U_EXP + 7, m)
                    for i in range(4, 6):
                        split(U_EXP + 10 + i, m)
                m, s = dve.snap(steps + (E_STEPS - 2)), dve.snap(steps + (E_STEPS - 1))
                for i in range(2):
                    split(U_EXP + 10 + i, m)
                down_lo(s)
                with dve.If(total > t + 1):
                    make_pick(t + 1)
                    split(U_EXP + E_UNITS, steps)
                    split(U_EXP + E_UNITS + 1, steps)
                activate(s + 1, U_EXP + 7, m)
                down_lo(steps + E_STEPS)
                with dve.If(total > t + 1):
                    split(U_EXP + E_UNITS + 2, steps)
                    gathered_lo(t + 2)
                    split(U_EXP + E_UNITS + 3, steps)
                for h in range(2):
                    dve.wait_ge(e_y_hi, t * 2 + (h + 1))
                    V.tensor_tensor(y_s[1][:, h * 512:(h + 1) * 512], bank[3 + h][:],
                                    y_s[0][:, h * 512:(h + 1) * 512].bitcast(F32), SUB).then_inc(e_y_lo, 1)
                with dve.If(total > t + 1):
                    split(U_EXP + E_UNITS + 4, steps)
                    split(U_EXP + E_UNITS + 5, steps)
                for h in range(2):
                    for b in range(TB):
                        dve.wait_ge(scattered, t * 4 + (2 * h + b + 1))
                        xo = x[:, b, h * 512:(h + 1) * 512]
                        V.scalar_tensor_tensor(xo, bank[(6, 7, 5, 2)[2 * h + b]][:],
                                               route[:, bass.ds(t + (128 + 16 * b), 1)], xo,
                                               MUL, ADD).then_inc(x_added, 1)
            dve.wait_ge(root_ready, 6)
            dve.wait_ge(final_gain_loaded, 16)
            then(V.reciprocal(stats[:, 10:12], stats[:, 10:12]))
            for t in range(TB):
                ins = V.scalar_tensor_tensor(out_sb[:, t, :], x[:, t, :], stats[:, 10 + t:11 + t], final_gain[:],
                                             MUL, MUL)
            ins.then_inc(normed, 1)


_INS = ["x", "mem", "positions", "mix_norm", "w_in_a", "gla_gate_w", "gla_gate_b", "gla_out_norm", "w_in_b",
        "swa_sinks", "mem_norm", "w_mem_kv", "w_out", "ffn_norm", "ffn_w_gate_up", "ffn_w_down", "router_w",
        "exp_w_gate_up", "exp_w_down", "final_norm"]


def kernel(**inputs):
    import numpy as _np
    import concourse.bacc as _bacc
    from concourse import mybir as _mybir
    from concourse.bass_utils import run_bass_kernel_spmd as _run

    nc = _bacc.Bacc("TRN2", target_bir_lowering=False, num_devices=1)
    arrays, args = {}, []
    for name in _INS:
        a = _np.ascontiguousarray(inputs[name])
        arrays[f"in_{name}"] = a
        args.append(nc.dram_tensor(f"in_{name}", a.shape, _mybir.dt.from_np(a.dtype), kind="ExternalInput").ap())
    res = nc.dram_tensor("out_x", (1, TOK, D), F32, kind="ExternalOutput").ap()
    build(nc, *args, res)
    r = _run(nc, [arrays], core_ids=[0])
    return r.results[0]["out_x"]
```

```python
import math
from contextlib import ExitStack

import numpy as np

import concourse.bass as bass
import concourse.mybir as mybir

F32 = mybir.dt.float32
F32R = mybir.dt.float32r
I32 = mybir.dt.int32
U32 = mybir.dt.uint32
ALU = mybir.AluOpType
ACT = mybir.ActivationFunctionType
AX = mybir.AxisListType

P = 128
D = 1024
KT = D // P
TOK = 256
TB = TOK // P
HD = 64
MEM_W = 256
MAIN_W = D - MEM_W
GH, GDV, GDK, LOWRANK = 4, 192, 96, 16
GQK = GH * GDK
GLA_TAU, GLA_CHUNK = 16.0, 64
WINDOW = 128
SH, SKV = 12, 4
ROPE_HALF = 8
ROPE_THETA = 500000.0
F_DENSE = 2816
F_STEP = 256
F_STEPS = F_DENSE // F_STEP
NE, F_EXP = 8, 3584
E_STEP = 512
E_STEPS = F_EXP // E_STEP
ROUNDS = TOK // P
EPS = 1e-6
MASKED = -1e30

RAW, SPLIT = 3, 6
UNIT = 2048

A_V, A_GLR, A_R, A_QM = 2 * GQK, 2 * GQK + MAIN_W, 2 * GQK + MAIN_W + LOWRANK, 2 * GQK + 2 * MAIN_W + LOWRANK
B_QK = (SH + SKV) * HD

U_A0, U_KV0, U_A1, U_A2, U_KV1, U_A3, U_AQM, U_A4 = 0, 2, 4, 6, 8, 10, 12, 13
U_OUT0 = 15
U_FFN = 19
U_B0 = U_FFN + 3 * F_STEPS
U_BQM, U_B1, U_BV, U_OUT1 = U_B0 + 2, U_B0 + 3, U_B0 + 5, U_B0 + 6
U_EXP = U_OUT1 + 4
E_UNITS = 6 * E_STEPS
OUT_PAIRS = [3, 0, 1, 2]
Q_PAIRS = [(0, 3), (1, 4), (2, 5), (6, 9), (7, 10), (8, 11)]
Q_ORDER = [h for pair in Q_PAIRS for h in pair]
GROUP = 4
GLA_KV = [(1, 2), (3, 4), (0, 5)]
GLA_O = [(1, 2), (3, 4)]
OUT_BANKS = (0, 5, 6, 7)
FFN_BANKS = (0, 1, 2, 3)
SWA_O = (4, 1, 4)


def build(nc, x_in, mem_in, positions, mix_norm, w_in_a, gla_gate_w, gla_gate_b, gla_out_norm, w_in_b,
          swa_sinks, mem_norm, w_mem_kv, w_out, ffn_norm, ffn_w_gate_up, ffn_w_down, router_w,
          exp_w_gate_up, exp_w_down, final_norm, out):
    ctx = ExitStack()
    with ctx:
        place = [16512]

        def sb_at(name, shape, dt, offset):
            return nc.alloc_sbuf_tensor_at(name, shape, dt, offset=offset)

        def sb(name, shape, dt=F32):
            offset = place[0]
            place[0] += (int(np.prod(shape[1:])) * 4 + 31) // 32 * 32
            return sb_at(name, shape, dt, offset)

        def sem(name):
            return ctx.enter_context(nc.semaphore(name))

        assert WINDOW == P
        raw = [sb(f"weights_raw{i}", [P, UNIT]) for i in range(RAW)]
        whi = [sb(f"weights_hi{i}", [P, UNIT], F32R) for i in range(SPLIT)]
        wlo = [sb(f"weights_lo{i}", [P, UNIT], F32R) for i in range(SPLIT)]
        x = sb("x", [P, TB, D])
        hT_at = place[0]
        hT = [sb("hT_hi", [P, KT, TOK], F32R), sb("hT_lo", [P, KT, TOK], F32R)]
        mT_at = place[0]
        mT = [sb("mT_hi", [P, KT, TOK], F32R), sb("mT_lo", [P, KT, TOK], F32R)]
        kmT = [sb(f"mem_kT{l}", [P, 2, TOK]) for l in range(2)]
        vm = [sb(f"mem_v{l}", [P, TB, MEM_W]) for l in range(2)]
        qmT_at = place[0]
        qmT = sb("mem_qT", [P, 2, TOK])
        glrT = sb_at("gla_lowrankT", [LOWRANK + 1, TOK], F32, qmT_at)
        ident = sb("ident", [P, P])
        cum_m = sb("cum_matrix", [P, P])
        rem_m = sb("rem_matrix", [P, P])
        causal = sb("causal_chunks", [P, P])
        before = sb("before_matrix", [P, P])
        ones = sb("ones", [P, P])
        window = sb("window_mask", [P, 3 * P])
        iota = sb("iota", [P, P])
        gains = sb("gains", [P, 48])
        gate_w_at = place[0]
        gate_w = sb("gate_w", [LOWRANK + 1, GQK])
        route = sb_at("route", [P, 256], F32, gate_w_at)
        gla_gain = sb("gla_gain", [P, GDV])
        router_raw = sb("router_raw", [P, KT, NE])
        sinks = sb("sinks", [P, SH])
        pos_i = sb("pos_i", [P, TB], I32)
        stats = sb("stats", [P, 64])
        rope_c = sb("rope_c", [P, 8, TB * ROPE_HALF])
        swa = sb("swa_stats", [P, 4, TB * SH])
        sinks_at = sb("sinks_by_place", [P, TB * SH])
        small = sb("small", [P, 64])
        gate_now = sb("gate_now", [P, TB])
        route_u = sb("route_u", [P, TB, 8], U32)
        rounds_i = sb("rounds_i", [1, 1], I32)
        E0 = place[0]
        xT = sb_at("xT", [P, KT, TOK], F32, hT_at)
        xn = sb_at("xn", [P, TB, D], F32, E0)
        squares_of_mem = sb_at("squares_of_mem", [P, TB, D], F32, E0 + 8192)
        z = sb_at("gla_z", [P, TB, A_QM], F32, E0)
        E1 = E0 + TB * A_QM * 4
        memn = sb_at("memn", [P, TB, D], F32, E1)
        gain_rows = sb_at("gain_rows", [48, P], F32, E1 + 8192)
        ex = [sb_at(f"gla_exp{i}", [P, TB, GQK], F32, E1 + i * 3072) for i in range(3)]
        attn = sb_at("gla_attn", [P, TB, GH, P], F32, E1)
        la = sb_at("gla_log_alpha", [P, TB, GQK], F32, mT_at + 8192 + 3072)
        abs_g = sb_at("gla_abs_gate", [P, TB, GQK], F32, E1)
        ln_g = sb_at("gla_ln_gate", [P, TB, GQK], F32, E1 + 3072)
        state = [sb_at(f"gla_state{i}", [GDK, GH, GDV], F32, mT_at + a) for i, a in enumerate((0, 3072, 8192))]
        mp = sb_at("mem_probs", [P, TB, 2, 2, TOK], F32, mT_at)
        mpT = sb_at("mem_probsT", [P, 2, 2, TB, TOK], F32, hT_at + 8192)
        o_squares = sb_at("gla_squares", [P, GH, GDV], F32, hT_at + 8192)
        qdT = sb_at("gla_qT", [GDK, TB, GH, P], F32, hT_at)
        kdT = sb_at("gla_kT", [GDK, TB, GH, P], F32, hT_at + 4096)
        f_silu = [sb_at(f"ffn_silu{i}", [P, 2 * TOK], F32, E0 + 8192 + i * 2048) for i in range(2)]
        f_act = [sb_at(f"ffn_act{i}", [P, 2 * TOK], F32, E0 + 12288 + i * 2048) for i in range(2)]
        f_aT = [[sb_at(f"ffn_aT{i}_{h}", [P, 2, TOK], F32R, E0 + 16384 + i * 4096 + h * 2048) for h in range(2)]
                for i in range(2)]
        qk = sb_at("swa_qk", [P, TB, SH + SKV, HD], F32, E0)
        v_sb = vm[0]
        S = sb_at("swa_scores", [P, SH, 3 * P], F32, E0 + 8192)
        rope = [sb_at(f"rope{i}", [P, TB, SH + SKV, ROPE_HALF], F32, E0 + 8192 + i * 1024) for i in range(4)]
        qkT = sb_at("swa_qkT", [P, KT, TOK], F32, hT_at)
        spT = [sb_at(f"swa_probsT{i}", [P, 3 * P], F32, E0 + i * 1536) for i in range(4)]
        pick = sb_at("pick", [P, TB, P], F32, E0 + 8192)
        pickT = sb_at("pickT", [P, TOK], F32R, E0 + 9216)
        ffn_gain = sb_at("expert_gain", [P, D], F32, E0 + 14336)
        y_scaled = [sb_at(f"expert_y{i}", [P, 512], F32, E0 + 18432 + 2048 * i) for i in range(2 * TB)]
        e_silu = sb_at("expert_silu", [P, E_STEP], F32, E0 + 10240)
        e_act = sb_at("expert_act", [P, E_STEP], F32, E0 + 12288)
        e_aT = [hT[h][:, 0:4, P:TOK] for h in range(2)]
        y_s = [mT[h][:, 0:4, :].rearrange("p a b -> p (a b)") for h in range(2)]
        final_gain = sb_at("final_gain", [P, D], F32, mT_at + 8192 + 4096)
        out_sb = sb_at("out_sb", [P, TB, D], F32, E0 + 14336)
        assert E1 + 9216 <= 229368, E0

        o_sb = z[:, :, 0:MAIN_W].rearrange("p t (h v) -> p t h v", h=GH)
        bank = [ctx.enter_context(nc.psum_tensor(f"bank{i}", [P, 512], F32)) for i in range(8)]

        x_loaded, mem_loaded, params_loaded = sem("x_loaded"), sem("mem_loaded"), sem("params_loaded")
        gains_loaded = sem("gains_loaded")
        final_gain_loaded, ffn_gain_loaded = sem("final_gain_loaded"), sem("ffn_gain_loaded")
        out_written = sem("out_written")
        weights_landed = [sem(f"weights_landed{i}") for i in range(RAW)]
        weights_hi, weights_lo, weights_used = sem("weights_hi"), sem("weights_lo"), sem("weights_used")
        ident_ready, consts = sem("ident_ready"), sem("consts")
        pool_chain, act_chain, dve_chain = sem("pool_chain"), sem("act_chain"), sem("dve_chain")
        gains_turned, gains_ready = sem("gains_turned"), sem("gains_ready")
        root_ready = sem("root_ready")
        scales_ready = sem("scales_ready")
        normed = sem("normed")
        turned = sem("turned")
        turned_hi, turned_lo = sem("turned_hi"), sem("turned_lo")
        kv_act, kv_dve = sem("kv_act"), sem("kv_dve")
        proj_act, proj_dve = sem("proj_act"), sem("proj_dve")
        mscore, mmax, mprob, mnorm = sem("mem_scores"), sem("mem_max"), sem("mem_probs"), sem("mem_norm")
        mturn, mturned_a, mturned_d = sem("mem_probs_turned"), sem("mem_probsT_act"), sem("mem_probsT_dve")
        mout, mout_hi, mout_lo = sem("mem_out"), sem("mem_out_hi"), sem("mem_out_lo")
        glr_turned, glr_ready, gate_logits = sem("glr_turned"), sem("glr_ready"), sem("gate_logits")
        ln_ready, la_ready = sem("ln_ready"), sem("la_ready")
        cum_done, gexp = sem("cum_done"), sem("gla_exps")
        decay_done, decay_ready = sem("decay_done"), sem("decay_ready")
        gdec, gturn = sem("gla_decayed"), sem("gla_qk_turned")
        gturned_q, gturned_k = sem("gla_qT_ready"), sem("gla_kT_ready")
        gattn, gattn_ready = sem("gla_attn_done"), sem("gla_attn_ready")
        gkv, gstate = sem("gla_kv"), sem("gla_state")
        go = sem("gla_o_done")
        silu_r, oroot, onorm = sem("silu_r"), sem("gla_o_root"), sem("gla_o_normed")
        mainT, mainT_hi, mainT_lo = sem("mainT"), sem("mainT_hi"), sem("mainT_lo")
        y_act, y_dve = sem("y_act"), sem("y_dve")
        f_silu_ready, f_act_ready = sem("ffn_silu_ready"), sem("ffn_act_ready")
        f_hi, f_lo = sem("ffn_aT_hi"), sem("ffn_aT_lo")
        angles, sincos, roped = sem("angles"), sem("sincos"), sem("roped")
        sturn, sturned_a, sturned_d = sem("swa_turn"), sem("swa_turned_act"), sem("swa_turned_dve")
        sscore, sscaled = sem("swa_scores"), sem("swa_scaled")
        smax, sprob, snorm = sem("swa_max"), sem("swa_probs"), sem("swa_normed")
        sgap, ssink = sem("swa_sink_gap"), sem("swa_sink_exp")
        spturn, spturned_a, spturned_d = sem("swa_pT"), sem("swa_pT_act"), sem("swa_pT_dve")
        sout = sem("swa_out")
        xT_act, xT_dve = sem("xT_act"), sem("xT_dve")
        logits = sem("logits")
        gap_ready, gap_exp = sem("gap_ready"), sem("gap_exp")
        mask_ready, ranks, routed = sem("mask_ready"), sem("ranks"), sem("routed")
        pick_made, pick_turned, pickT_ready = sem("pick_made"), sem("pick_turned"), sem("pickT_ready")
        gathered, gath_hi, gath_lo = sem("gathered"), sem("gathered_hi"), sem("gathered_lo")
        e_silu_ready, e_act_ready = sem("expert_silu"), sem("expert_act")
        e_turned, e_hi, e_lo = sem("expert_turned"), sem("expert_aT_hi"), sem("expert_aT_lo")
        e_y_hi, e_y_lo = sem("expert_y_hi"), sem("expert_y_lo")
        gate_ready = sem("gate_ready")
        scattered, x_added, x_final = sem("scattered"), sem("x_added"), sem("x_final")
        y_weighted_act, y_weighted_dve = sem("y_weighted_act"), sem("y_weighted_dve")

        def tiles(ap, k0, nk, c0, w):
            return ap[k0 * P:(k0 + nk) * P, c0:c0 + w].rearrange("(k p) c -> p k c", p=P)

        wa, wb, wo = w_in_a[0], w_in_b[0], [w_out[0], w_out[1]]
        wgu, wdn = ffn_w_gate_up[0], ffn_w_down[0]
        halves = lambda ap, c0, w: [tiles(ap, 0, 4, c0, w), tiles(ap, 4, 4, c0, w)]
        units = halves(wa, 1536, 512) + halves(w_mem_kv[0], 0, 512)
        units += halves(wa, 0, 512) + halves(wa, 512, 512) + halves(w_mem_kv[1], 0, 512)
        units += halves(wa, 1024, 512) + [tiles(wa, 0, 8, A_QM, MEM_W)]
        units += halves(wa, 2048, A_QM - 2048)
        units += [tiles(wo[0], 2 * p, 2, 0, D) for p in OUT_PAIRS]
        assert len(units) == U_FFN
        ffn_gu = [tiles(wgu, 0, 8, 0, F_STEP), tiles(wgu, 0, 8, F_DENSE, F_STEP)]
        tail = halves(wb, 0, 512) + [tiles(wb, 0, 8, B_QK + SKV * HD, MEM_W)]
        tail += halves(wb, 512, 512) + [tiles(wb, 0, 8, B_QK, SKV * HD)]
        tail += [tiles(wo[1], 2 * p, 2, 0, D) for p in OUT_PAIRS]
        assert U_B0 + len(tail) == U_EXP

        def unit_view(buf, nk, w):
            return buf[:, 0:nk * w].rearrange("p (k c) -> p k c", k=nk)

        def halves_of(words):
            return [slice(0, words // 2), slice(words // 2, words)]

        def size(n):
            return 4 * (A_QM - 2048) if n in (U_A4, U_A4 + 1) else UNIT

        def qk_pieces(t, half, b):
            src = b[:].rearrange("p (h d) -> p h d", d=HD)
            if half == 0:
                return [(qk[:, t, 0:6].rearrange("p (j r) d -> p r j d", r=2),
                         src[:, 0:6].rearrange("p (r j) d -> p r j d", r=2)), (qk[:, t, 6:9:2], src[:, 6:8])]
            return [(qk[:, t, 10:11], src[:, 0:1]), (qk[:, t, 7:12:2], src[:, 1:4]), (qk[:, t, 12:16], src[:, 4:8])]

        block = ctx.enter_context(nc.Block())

        @block.sync
        def _(sp):
            for i, g in enumerate((mix_norm, mem_norm, ffn_norm)):
                sp.dma_start(gain_rows[16 * i:16 * i + 16, :],
                             g.rearrange("l (k p) -> (l k) p", p=P)).then_inc(gains_loaded, 16)
            sp.dma_start(x[:], x_in[0].rearrange("(t p) d -> p t d", p=P)).then_inc(x_loaded, 16)

            def load(n, slot_n, src):
                nk, w = src.shape[1], src.shape[2]
                if not isinstance(n, int) or n >= RAW:
                    sp.wait_ge(weights_lo, n - RAW + 1)
                sp.dma_start(unit_view(raw[slot_n % RAW], nk, w), src).then_inc(weights_landed[slot_n % RAW], 16)

            for n, src in enumerate(units):
                load(n, n, src)
                if n == 0:
                    sp.dma_start(memn[:], mem_in[0].rearrange("(t p) d -> p t d", p=P)).then_inc(mem_loaded, 16)
            load(U_FFN, U_FFN, ffn_gu[0])
            load(U_FFN + 1, U_FFN + 1, ffn_gu[1])
            with sp.Fori(1, F_STEPS) as j:
                n = U_FFN - 1 + j * 3
                cols = bass.ds(j * F_STEP, F_STEP)
                load(n, U_FFN + 2, wgu[:, cols].rearrange("(k p) c -> p k c", p=P))
                cols = bass.ds(j * F_STEP + F_DENSE, F_STEP)
                load(n + 1, U_FFN + 3, wgu[:, cols].rearrange("(k p) c -> p k c", p=P))
                rows = wdn.rearrange("(j k p) c -> j p k c", p=P, k=2)
                load(n + 2, U_FFN + 4, rows[j - 1])
            load(U_B0 - 1, U_B0 - 1, wdn[F_DENSE - F_STEP:F_DENSE, :].rearrange("(k p) c -> p k c", p=P))
            for i, src in enumerate(tail):
                load(U_B0 + i, U_B0 + i, src)

            down = exp_w_down[0].rearrange("e (j u k p) c -> e j u p k c", u=2, k=2, p=P)

            def load_experts(r):
                with sp.Fori(0, NE) as e:
                    base = sp.snap(e * E_UNITS + (r * NE * E_UNITS + U_EXP))

                    def gate_up(n, slot_n, j):
                        for i, (c0, k0) in enumerate(((0, 0), (0, 4), (F_EXP, 0), (F_EXP, 4))):
                            cols = bass.ds(j * E_STEP + c0, E_STEP)
                            src = exp_w_gate_up[0, e, k0 * P:(k0 + 4) * P, cols]
                            load(n + i, slot_n + i, src.rearrange("(k p) c -> p k c", p=P))

                    gate_up(base, U_EXP, 0)
                    with sp.Fori(1, E_STEPS) as j:
                        n = sp.snap(base + j * 6 - 2)
                        gate_up(n, U_EXP + 4, j)
                        load(n + 4, U_EXP + 8, down[e, j - 1, 0])
                        load(n + 5, U_EXP + 9, down[e, j - 1, 1])
                    load(base + (E_UNITS - 2), U_EXP + E_UNITS - 2, down[e, E_STEPS - 1, 0])
                    load(base + (E_UNITS - 1), U_EXP + E_UNITS - 1, down[e, E_STEPS - 1, 1])

            load_experts(0)
            sp.wait_ge(routed, 1)
            rounds = sp.value_load(rounds_i[0:1, 0:1], min_val=1, max_val=ROUNDS)
            with sp.If(rounds > 1):
                load_experts(1)

            for b in range(TB):
                sp.wait_ge(normed, 5 + b)
                sp.dma_start(out[0, b * P:(b + 1) * P, :], out_sb[:, b, :]).then_inc(out_written, 16)
            sp.wait_ge(out_written, 16 * TB)

        @block.gpsimd
        def _(pool):
            count = [0]

            def then(ins):
                count[0] += 1
                ins.then_inc(pool_chain, 1)
                pool.wait_ge(pool_chain, count[0])

            def select(ap, keep, fill, base, cm, step):
                return pool.affine_select(out=ap, in_=ap, compare_op=keep, fill=fill, base=base,
                                          pattern=[[step, ap.shape[1]]], channel_multiplier=cm)

            then(pool.memset(ident[:], 0.0))
            select(ident[:], ALU.not_equal, 1.0, 0, 1, -1).then_inc(ident_ready, 1)
            pool.dma_start(gate_w[0:LOWRANK, :], gla_gate_w[0]).then_inc(params_loaded, 16)
            pool.dma_start(gate_w[LOWRANK:LOWRANK + 1, :], gla_gate_b).then_inc(params_loaded, 16)
            pool.dma_start(gla_gain[:], gla_out_norm.partition_broadcast(P)).then_inc(params_loaded, 16)
            pool.dma_start(sinks[:], swa_sinks.partition_broadcast(P)).then_inc(params_loaded, 16)
            pool.dma_start(router_raw[:], router_w[0].rearrange("(k p) e -> p k e", p=P)).then_inc(params_loaded, 16)
            pool.dma_start(pos_i[:], positions[0].rearrange("(t p) -> p t", p=P),
                           allow_slow_non_contiguous=True).then_inc(params_loaded, 16)

            then(pool.memset(cum_m[:], 1.0 / GLA_TAU))
            then(select(cum_m[:], ALU.is_ge, 0.0, 0, -1, 1))
            then(pool.memset(cum_m[0:GLA_CHUNK, GLA_CHUNK:P], 0.0))
            then(pool.memset(rem_m[:], 1.0 / GLA_TAU))
            then(select(rem_m[:], ALU.is_ge, 0.0, -1, 1, -1))
            then(pool.memset(rem_m[GLA_CHUNK:P, 0:GLA_CHUNK], 0.0))
            then(pool.memset(causal[:], 1.0))
            then(select(causal[:], ALU.is_ge, 0.0, 0, -1, 1))
            then(pool.memset(causal[0:GLA_CHUNK, GLA_CHUNK:P], 0.0))
            then(pool.memset(before[:], 1.0))
            then(select(before[:], ALU.is_ge, 0.0, -1, -1, 1))
            then(pool.memset(window[:], 0.0))
            then(select(window[:, 0:P], ALU.is_ge, MASKED, 0, 1, -1))
            then(select(window[:, P:2 * P], ALU.is_ge, MASKED, -1, -1, 1))
            then(select(window[:, 2 * P:3 * P], ALU.is_ge, MASKED, 0, 1, -1))
            then(pool.iota(iota[:], pattern=[[1, P]], base=0, channel_multiplier=0,
                           allow_small_or_imprecise_dtypes=True))
            pool.memset(ones[:], 1.0).then_inc(consts, 1)

            pool.wait_ge(routed, 1)
            rounds = pool.value_load(rounds_i[0:1, 0:1], min_val=1, max_val=ROUNDS)
            with pool.Fori(0, pool.snap(rounds * NE - 1)) as t:
                for h in range(2):
                    for b in range(TB):
                        i = 2 * h + b
                        pool.wait_ge(y_weighted_act if b == 0 else y_weighted_dve, t * 2 + (h + 2))
                        xo = x[:, b, h * 512:(h + 1) * 512]
                        pool.tensor_tensor(xo, y_scaled[i][:], xo, ALU.add).then_inc(x_added, 1)

        @block.tensor
        def _(pe):
            mm = nc.tensor.matmul
            tr = nc.tensor.transpose

            def passes(psum, st, mv, first, last):
                mm(psum, st[0], mv[0], start=first, stop=False)
                mm(psum, st[1], mv[0], start=False, stop=False)
                return mm(psum, st[0], mv[1], start=False, stop=last)

            def unit(n, nk, w, m=0):
                pe.wait_ge(weights_lo, m * 6 + (n + 1))
                return [unit_view(b[n % SPLIT], nk, w) for b in (whi, wlo)]

            def to_T(src, y_count=None, whole_at=2):
                for b in range(4):
                    if y_count is not None and b in (0, whole_at):
                        pe.wait_ge(y_act, y_count - (b == 0))
                        pe.wait_ge(y_dve, y_count - (b == 0))
                    for k in (2 * b, 2 * b + 1):
                        for t in range(TB):
                            c = (k % 2) * TOK + t * P
                            ins = tr(bank[4 + b][:, c:c + P], src[:, t, k * P:(k + 1) * P], ident[:])
                    ins.then_inc(turned, 1)

            def project(n, k0, nk, w, st, banks, first, last, c0=0, cw=None):
                u = unit(n, nk, w)
                cw = w if cw is None else cw
                for k in range(nk):
                    for t in range(TB):
                        s = [a[:, k0 + k, t * P:(t + 1) * P] for a in st]
                        ins = passes(bank[banks[t]][:, 0:cw], s, [a[:, k, c0:c0 + cw] for a in u],
                                     first and k == 0, last and k == nk - 1)
                return ins

            def chunk(n, w, banks, turns=None):
                for i in range(2):
                    if turns is not None:
                        pe.wait_ge(turned_lo, turns + 2 * i + 2)
                    project(n + i, 4 * i, 4, w, hT, banks, i == 0, i == 1).then_inc(weights_used, 1)

            def mem_kv(n, banks):
                for h in range(2):
                    u = unit(n + h, 4, 512)
                    for k in range(4):
                        first, last = h == 0 and k == 0, h == 1 and k == 3
                        mem_k = [a[:, 4 * h + k, :] for a in mT]
                        for i in range(2):
                            passes(bank[banks[i]][:, 0:TOK], [a[:, k, i * P:(i + 1) * P] for a in u], mem_k,
                                   first, last)
                        for t in range(TB):
                            ins = passes(bank[banks[2 + t]][:, 0:MEM_W], [a[:, t * P:(t + 1) * P] for a in mem_k],
                                         [a[:, k, MEM_W:2 * MEM_W] for a in u], first, last)
                    ins.then_inc(weights_used, 1)

            def mem_query(n, banks):
                u = unit(n, KT, MEM_W)
                for i in range(2):
                    for k in range(KT):
                        ins = passes(bank[banks[i]][:, 0:TOK], [a[:, k, i * P:(i + 1) * P] for a in u],
                                     [a[:, k, :] for a in hT], k == 0, k == KT - 1)
                ins.then_inc(weights_used, 1)

            def mem_scores():
                for t in range(TB):
                    for par in range(2):
                        for i in range(2):
                            r = slice(par * HD, (par + 1) * HD)
                            ins = mm(bank[1 + 2 * t + par][:, i * TOK:(i + 1) * TOK],
                                     qmT[r, i, t * P:(t + 1) * P], kmT[layer[0]][r, i, :], start=True, stop=True)
                    ins.then_inc(mscore, 1)

            def mem_turn():
                for t in range(TB):
                    pe.wait_ge(mnorm, 2 * layer[0] + t + 1)
                    for par in range(2):
                        b = bank[1 + 2 * t + par]
                        for i in range(2):
                            for mb in range(TB):
                                c = (2 * i + mb) * P
                                ins = tr(b[:, c:c + P], mp[:, t, par, i, mb * P:(mb + 1) * P], ident[:])
                        ins.then_inc(mturn, 1)

            def mem_outputs(b):
                pe.wait_ge(mturned_a, 2 * layer[0] + 2)
                pe.wait_ge(mturned_d, 2 * layer[0] + 2)
                for par in range(2):
                    for i in range(2):
                        for mb in range(TB):
                            h = 2 * i + par
                            ins = mm(bank[b][par * HD:(par + 1) * HD, i * TOK:(i + 1) * TOK],
                                     vm[layer[0]][:, mb, h * HD:(h + 1) * HD], mpT[:, par, i, mb, :],
                                     start=(mb == 0), stop=(mb == TB - 1))
                ins.then_inc(mout, 1)

            def seed(banks):
                for t in range(TB):
                    for h in range(2):
                        mm(bank[banks[2 * t + h]][:], ident[:], x[:, t, h * 512:(h + 1) * 512], start=True, stop=False)

            def rows_product(u, k_of, st, banks, last):
                for i in range(2):
                    for t in range(TB):
                        for h in range(2):
                            s = [a[:, k_of + i, t * P:(t + 1) * P] for a in st]
                            ins = passes(bank[banks[2 * t + h]][:], s, [a[:, i, h * 512:(h + 1) * 512] for a in u],
                                         False, last and i == 1)
                return ins

            def start_out(n):
                seed(OUT_BANKS)
                pe.wait_ge(mout_lo, layer[0] + 1)
                rows_product(unit(n, 2, D), 6, mT, OUT_BANKS, False).then_inc(weights_used, 1)

            def finish_out(n):
                for pair in range(3):
                    pe.wait_ge(mainT_lo, 3 * layer[0] + pair + 1)
                    ins = rows_product(unit(n + 1 + pair, 2, D), 2 * pair, mT, OUT_BANKS, pair == 2)
                    ins.then_inc(weights_used, 1)

            layer = [0]
            pe.wait_ge(ident_ready, 1)
            pe.wait_ge(gains_loaded, 16 * 3)
            tr(bank[0][:, 0:48], gain_rows[:], ident[0:48, 0:48]).then_inc(gains_turned, 1)
            pe.wait_ge(x_loaded, 16)
            to_T(x)
            pe.wait_ge(gains_ready, 1)
            pe.wait_ge(turned_lo, 2)
            project(U_A0, 0, 4, 512, hT, (0, 1), True, False).then_inc(weights_used, 1)
            pe.wait_ge(turned_lo, 4)
            pe.wait_ge(normed, 1)
            to_T(memn)
            project(U_A0 + 1, 4, 4, 512, hT, (0, 1), False, True).then_inc(weights_used, 1)
            pe.wait_ge(turned_lo, 8)
            mem_kv(U_KV0, (4, 5, 6, 7))
            chunk(U_A1, 512, (2, 3))
            pe.wait_ge(kv_act, 1)
            pe.wait_ge(kv_dve, 1)
            pe.wait_ge(proj_act, 1)
            pe.wait_ge(proj_dve, 1)
            for t in range(TB):
                ins = tr(bank[0][0:LOWRANK, t * P:(t + 1) * P], z[:, t, A_GLR:A_GLR + LOWRANK], ident[:])
            ins.then_inc(glr_turned, 1)
            to_T(memn)
            pe.wait_ge(glr_ready, 1)
            chunk(U_A2, 512, (0, 1))
            pe.wait_ge(proj_act, 2)
            pe.wait_ge(proj_dve, 2)
            pe.wait_ge(params_loaded, 16 * 6)
            for t in range(TB):
                ins = mm(bank[2 + t][:, 0:GQK], glrT[:, t * P:(t + 1) * P], gate_w[:], start=True, stop=True)
                ins.then_inc(gate_logits, 1)
            pe.wait_ge(turned_lo, 12)
            mem_kv(U_KV1, (4, 5, 6, 7))
            pe.wait_ge(proj_act, 3)
            pe.wait_ge(proj_dve, 3)
            chunk(U_A3, 512, (0, 1))
            pe.wait_ge(consts, 1)
            pe.wait_ge(kv_act, 2)
            pe.wait_ge(kv_dve, 2)
            for t in range(TB):
                pe.wait_ge(la_ready, t + 1)
                for i, m in enumerate((cum_m, rem_m)):
                    ins = mm(bank[4 + 2 * t + i][:, 0:GQK], m[:], la[:, t, :], start=True, stop=True)
                ins.then_inc(cum_done, 1)
            mem_query(U_AQM, (2, 3))
            pe.wait_ge(proj_act, 4)
            pe.wait_ge(proj_dve, 4)
            pe.wait_ge(gexp, 3)
            chunk(U_A4, A_QM - 2048, (0, 5))

            pe.wait_ge(proj_act, 5)
            pe.wait_ge(proj_dve, 5)
            pe.wait_ge(gexp, 6)
            mem_scores()
            pe.wait_ge(proj_act, 6)
            pe.wait_ge(proj_dve, 6)
            for i, (t, r) in enumerate(((0, slice(GLA_CHUNK, P)), (1, slice(0, GLA_CHUNK)))):
                for h in range(GH):
                    ins = mm(bank[7 * (1 - i)][0:GDK, h:h + 1], la[r, t, h * GDK:(h + 1) * GDK],
                             cum_m[r, P - 1:P] if i == 0 else cum_m[r, GLA_CHUNK - 1:GLA_CHUNK],
                             start=True, stop=True)
            ins.then_inc(decay_done, 1)
            for t in range(TB):
                pe.wait_ge(gdec, 3 * t + 3)
                for i in range(2):
                    if t == 1:
                        pe.wait_ge(decay_ready, i + 1)
                    for h in range(GH):
                        ins = tr(bank[(5, 6, 7, 0)[2 * t + i]][0:GDK, h * P:(h + 1) * P],
                                 z[:, t, i * GQK + h * GDK:i * GQK + (h + 1) * GDK], ident[:])
                    ins.then_inc(gturn, 1)
            mem_turn()
            for t in range(TB):
                pe.wait_ge(gturned_q, t + 1)
                pe.wait_ge(gturned_k, t + 1)
                for h in range(GH):
                    ins = mm(bank[5 + t][:, h * P:(h + 1) * P], kdT[:, t, h, :], qdT[:, t, h, :], start=True, stop=True)
                ins.then_inc(gattn, 1)
            mem_outputs(7)
            for c in range(3):
                t, r = c // 2, slice(c % 2 * GLA_CHUNK, (c % 2 + 1) * GLA_CHUNK)
                if c == 2:
                    pe.wait_ge(gattn_ready, 1)
                for h in range(GH):
                    ins = mm(bank[GLA_KV[c][h // 2]][0:GDK, (h % 2) * GDV:(h % 2 + 1) * GDV],
                             ex[2][r, t, h * GDK:(h + 1) * GDK], z[r, t, A_V + h * GDV:A_V + (h + 1) * GDV],
                             start=True, stop=True)
                ins.then_inc(gkv, 1)
            for t in range(TB):
                pe.wait_ge(gattn_ready, t + 1)
                pe.wait_ge(gstate, 2 * t + 1)
                for h in range(GH):
                    o = bank[GLA_O[t][h // 2]][:, (h % 2) * GDV:(h % 2 + 1) * GDV]
                    ins = mm(o, attn[:, t, h, :], z[:, t, A_V + h * GDV:A_V + (h + 1) * GDV],
                             start=True, stop=False, skip_group_check=True)
                    for c in (1,) if t == 0 else (2, 3):
                        r = slice(c % 2 * GLA_CHUNK, (c % 2 + 1) * GLA_CHUNK)
                        ins = mm(o[r, :], qdT[:, t, h, r], state[c - 1][:, h, :], start=False, stop=True,
                                 skip_group_check=True)
                ins.then_inc(go, 1)
            pe.wait_ge(mout_lo, 1)
            start_out(U_OUT0)
            pe.wait_ge(onorm, 2)
            for b in range(3):
                for k in (2 * b, 2 * b + 1):
                    for t in range(TB):
                        c = (k % 2) * TOK + t * P
                        ins = tr(bank[1 + b][:, c:c + P], z[:, t, k * P:(k + 1) * P], ident[:])
                ins.then_inc(mainT, 1)
            finish_out(U_OUT0)
            layer[0] = 1

            pe.wait_ge(y_act, 2)
            pe.wait_ge(y_dve, 2)
            seed(FFN_BANKS)
            pe.wait_ge(normed, 2)
            to_T(xn)

            def gate_up(n, par, m, turns=None):
                for i in range(2):
                    u = unit(n + i, KT, F_STEP, m)
                    for f in range(2):
                        for k in range(KT):
                            if turns is not None and i == 0 and f == 0 and k % 2 == 0:
                                pe.wait_ge(turned_lo, turns + k // 2 + 1)
                            ins = passes(bank[4 + 2 * par + i][:, f * TOK:(f + 1) * TOK],
                                         [a[:, k, f * P:(f + 1) * P] for a in u], [a[:, k, :] for a in hT],
                                         k == 0, k == KT - 1)
                    ins.then_inc(weights_used, 1)

            def ffn_down(n, par, m, last=False):
                rows_product(unit(n, 2, D, m), 0, f_aT[par], FFN_BANKS, last).then_inc(weights_used, 1)

            gate_up(U_FFN, 0, 0, 12)
            with pe.Fori(0, (F_STEPS - 1) // 2) as i:
                for s in range(2):
                    j0 = s + 1
                    pe.wait_ge(f_act_ready, i * 2 + j0)
                    gate_up(U_FFN + 2 + 3 * s, j0 % 2, i)
                    pe.wait_ge(f_lo, i * 2 + (s + 1))
                    ffn_down(U_FFN + 4 + 3 * s, (j0 - 1) % 2, i)
            pe.wait_ge(f_lo, F_STEPS)
            ffn_down(U_B0 - 1, 0, 0, True)

            to_T(x, 4)
            chunk(U_B0, 512, (0, 1), 16)
            mem_query(U_BQM, (2, 3))
            chunk(U_B1, 512, (5, 6))
            pe.wait_ge(proj_act, 8)
            pe.wait_ge(proj_dve, 8)
            mem_scores()
            project(U_BV, 0, KT, SKV * HD, hT, (7, 0), True, True).then_inc(weights_used, 1)
            pe.wait_ge(roped, 1)
            for b in range(4):
                if b == 2:
                    pe.wait_ge(proj_act, 10)
                    pe.wait_ge(proj_dve, 10)
                for i in range(2):
                    j = 2 * b + i
                    for t in range(TB):
                        src = qk[:, t, 2 * j:2 * j + 2, :].rearrange("p h d -> p (h d)")
                        ins = tr(bank[(5, 6, 7, 0)[b]][:, i * TOK + t * P:i * TOK + (t + 1) * P], src, ident[:])
                ins.then_inc(sturn, 1)
            mem_turn()
            pe.wait_ge(sturned_a, 2)
            pe.wait_ge(sturned_d, 2)
            for j in range(6):
                if j == 2:
                    mem_outputs(1)
                if j >= 2:
                    pe.wait_ge(sscaled, 2 * (j - 1))
                for par in range(2):
                    r = slice(par * HD, (par + 1) * HD)
                    q, k = qkT[r, j, :], qkT[r, 6 + j // 3, :]
                    b = bank[(5, 6, 7, 0)[2 * (j % 2) + par]]
                    mm(b[:, 0:P], q[:, 0:P], k[:, 0:P], start=True, stop=True)
                    ins = mm(b[:, P:3 * P], q[:, P:TOK], k[:, 0:TOK], start=True, stop=True)
                    ins.then_inc(sscore, 1)
            pe.wait_ge(sscaled, SH)
            start_out(U_OUT1)
            for n in range(SH + 1):
                if n < SH:
                    if n % GROUP == 0:
                        pe.wait_ge(snorm, n // GROUP + 1)
                    if n >= 2:
                        pe.wait_ge(spturned_a if n % 2 == 0 else spturned_d, n // 2)
                    for i in range(3):
                        ins = tr(bank[2 + n % 2][:, i * P:(i + 1) * P], S[:, n, i * P:(i + 1) * P], ident[:])
                    ins.then_inc(spturn, 1)
                if n > 0:
                    m, h = n - 1, Q_ORDER[n - 1]
                    pe.wait_ge(spturned_a if m % 2 == 0 else spturned_d, m // 2 + 1)
                    if m == Q_ORDER.index(9):
                        pe.wait_ge(mainT_lo, 4)
                    kv = slice(h // 3 * HD, (h // 3 + 1) * HD)
                    o = bank[SWA_O[h // 4]][(h % 2) * HD:(h % 2 + 1) * HD, :]
                    c = h // 2 % 2 * TOK
                    mm(o[:, c:c + P], v_sb[:, 0, kv], spT[m % 4][:, 0:P], start=True, stop=True)
                    mm(o[:, c + P:c + TOK], v_sb[:, 0, kv], spT[m % 4][:, P:2 * P], start=True, stop=False)
                    ins = mm(o[:, c + P:c + TOK], v_sb[:, 1, kv], spT[m % 4][:, 2 * P:3 * P], start=False, stop=True)
                    ins.then_inc(sout, 1)
            finish_out(U_OUT1)

            to_T(x, 6, 1)
            for i, b in enumerate((1, 2, 3, 0)):
                if b == 0:
                    pe.wait_ge(xT_act, 1)
                else:
                    pe.wait_ge(xT_dve, b)
                for k in (2 * b, 2 * b + 1):
                    for t in range(TB):
                        ins = mm(bank[t][:, 0:NE], xT[:, k, t * P:(t + 1) * P], router_raw[:, k, :],
                                 start=(i == 0 and k % 2 == 0), stop=(i == 3 and k % 2 == 1))
            ins.then_inc(logits, 1)
            pe.wait_ge(mask_ready, 1)
            mask = [route[:, 64 + NE * t:64 + NE * (t + 1)] for t in range(TB)]
            mm(bank[2][:, 0:NE], before[:], mask[0], start=True, stop=True)
            mm(bank[3][:, 0:NE], ones[:], mask[0], start=True, stop=False)
            mm(bank[3][:, 0:NE], before[:], mask[1], start=False, stop=True)
            mm(bank[4][:, 0:NE], ones[:], mask[0], start=True, stop=False)
            mm(bank[4][:, 0:NE], ones[:], mask[1], start=False, stop=True).then_inc(ranks, 1)

            def expert_gate_up(i, n, m, gathers=None):
                for h in range(2):
                    if gathers is not None:
                        pe.wait_ge(gath_lo, gathers * 2 + (h - 1))
                    u = unit(n + 2 * i + h, 4, E_STEP, m)
                    for k in range(4):
                        ins = passes(bank[i][:], [a[:, 4 * h + k, 0:P] for a in hT], [a[:, k, :] for a in u],
                                     h == 0 and k == 0, h == 1 and k == 3)
                    ins.then_inc(weights_used, 1)

            def expert_turn():
                for i in range(4):
                    ins = tr(bank[2][:, i * P:(i + 1) * P], e_act[:, i * P:(i + 1) * P], ident[:])
                ins.then_inc(e_turned, 1)

            def expert_down(n, m, first, last):
                for i in range(2):
                    u = unit(n + i, 2, D, m)
                    for k in range(2):
                        for h in range(2):
                            ins = passes(bank[3 + h][:], [a[:, 2 * i + k, :] for a in e_aT],
                                         [a[:, k, h * 512:(h + 1) * 512] for a in u],
                                         first and i == 0 and k == 0, last and i == 1 and k == 1)
                    ins.then_inc(weights_used, 1)

            def gather(count):
                pe.wait_ge(pick_made, count)
                if isinstance(count, int):
                    pe.wait_ge(normed, 4)
                for k in range(KT):
                    for b in range(TB):
                        ins = mm(bank[6 + k // 4][:, k % 4 * P:(k % 4 + 1) * P], xn[:, b, k * P:(k + 1) * P],
                                 pick[:, b, :], start=(b == 0), stop=(b == 1))
                    if k % 4 == 3:
                        ins.then_inc(gathered, 1)

            def middle_step(s, m, first_of=None):
                pe.wait_ge(e_silu_ready, s)
                expert_gate_up(0, U_EXP + 4, m)
                pe.wait_ge(e_act_ready, s)
                if first_of is not None:
                    pe.wait_ge(pickT_ready, first_of)
                expert_turn()
                expert_gate_up(1, U_EXP + 4, m)
                pe.wait_ge(e_lo, s)
                expert_down(U_EXP + 8, m, first_of is not None, False)

            gather(1)
            expert_gate_up(0, U_EXP, 0, 1)
            pe.wait_ge(routed, 1)
            rounds = pe.value_load(rounds_i[0:1, 0:1], min_val=1, max_val=ROUNDS)
            total = pe.snap(rounds * NE)
            with pe.Fori(0, total) as t:
                steps = pe.snap(t * E_STEPS)
                expert_gate_up(1, U_EXP, steps)
                pe.wait_ge(y_weighted_act, t * 2 + 1)
                pe.wait_ge(y_weighted_dve, t * 2 + 1)
                for b in range(TB):
                    ins = tr(bank[2][:, b * P:(b + 1) * P], pick[:, b, :], ident[:])
                ins.then_inc(pick_turned, 1)
                middle_step(pe.snap(steps + 1), steps, t + 1)
                with pe.Fori(2, E_STEPS - 1) as j:
                    middle_step(pe.snap(steps + j), pe.snap(steps + (j - 1)))
                middle_step(pe.snap(steps + (E_STEPS - 1)), pe.snap(steps + (E_STEPS - 2)))
                pe.wait_ge(e_act_ready, steps + E_STEPS)
                expert_turn()
                with pe.If(total > t + 1):
                    gather(t + 2)
                pe.wait_ge(e_lo, steps + E_STEPS)
                expert_down(U_EXP + E_UNITS - 2, steps, False, True)
                with pe.If(total > t + 1):
                    expert_gate_up(0, U_EXP + E_UNITS, steps, t + 2)
                for h in range(2):
                    pe.wait_ge(e_y_lo, t * 2 + (h + 1))
                    for b in range(TB):
                        o = bank[(6, 7, 5, 2)[2 * h + b]]
                        mm(o[:], pickT[:, b * P:(b + 1) * P], y_s[0][:, h * 512:(h + 1) * 512],
                           start=True, stop=False)
                        ins = mm(o[:], pickT[:, b * P:(b + 1) * P], y_s[1][:, h * 512:(h + 1) * 512],
                                 start=False, stop=True)
                        ins.then_inc(scattered, 1)

        @block.scalar
        def _(act):
            A = nc.scalar.activation
            fed = [0]

            def split(n, m=0, words=UNIT):
                act.wait_ge(weights_landed[n % RAW], m * 32 + 16 * (n // RAW + 1))
                if not isinstance(m, int) or n >= SPLIT:
                    act.wait_ge(weights_used, m * 6 + (n - SPLIT + 1))
                for half in halves_of(words):
                    A(whi[n % SPLIT][:, half], raw[n % RAW][:, half], ACT.Copy).then_inc(weights_hi, 1)

            def feed(count):
                for _ in range(count):
                    split(fed[0], 0, size(fed[0]))
                    fed[0] += 1

            chain = [0]

            def then(ins):
                chain[0] += 1
                ins.then_inc(act_chain, 1)
                act.wait_ge(act_chain, chain[0])

            def squares(src, junk, col):
                for t in range(TB):
                    A(junk[:, t, :], src[:, t, :], ACT.Square,
                      accum_out=stats[:, col + t:col + t + 1]).then_inc(act_chain, 1)
                chain[0] += 2

            def root(col, count):
                act.wait_ge(act_chain, chain[0])
                A(stats[:, col:col + count], stats[:, col:col + count], ACT.Sqrt, bias=EPS,
                  scale=1.0 / D).then_inc(root_ready, 1)

            def root_mean_square(src, junk, col):
                squares(src, junk, col)
                root(col, 2)

            def scaled_out(dst, b, last_unit, count, col):
                act.wait_ge(weights_used, last_unit + 1)
                act.wait_ge(scales_ready, count)
                A(dst, b, ACT.Copy, scale=stats[:, col:col + 1]).then_inc(proj_act, 1)

            def kv_out(l, last_unit):
                act.wait_ge(weights_used, last_unit + 1)
                for i in range(2):
                    ins = A(kmT[l][:, i, :], bank[4 + i][:, 0:TOK], ACT.Copy)
                ins.then_inc(kv_act, 1)

            def turned_hi_of(dst, call, gain_col, banks=range(4)):
                for b in banks:
                    act.wait_ge(turned, 4 * call + b + 1)
                    for i in range(2):
                        k = 2 * b + i
                        ins = A(dst[:, k, :], bank[4 + b][:, i * TOK:(i + 1) * TOK], ACT.Copy,
                                scale=gains[:, gain_col + k:gain_col + k + 1])
                    ins.then_inc(turned_hi, 1)

            def chunk_out(dst, b, last_unit):
                act.wait_ge(weights_used, last_unit + 1)
                A(dst, b, ACT.Copy).then_inc(proj_act, 1)

            def qk_out(half, b, last_unit):
                act.wait_ge(weights_used, last_unit + 1)
                act.wait_ge(scales_ready, 2)
                for dst, src in qk_pieces(0, half, b):
                    ins = A(dst, src, ACT.Copy, scale=stats[:, 6:7])
                ins.then_inc(proj_act, 1)

            def mem_probs(l, col, t):
                act.wait_ge(mmax, 2 * l + t + 1)
                for par in range(2):
                    for i in range(2):
                        c = 4 * t + 2 * par + i
                        ins = A(mp[:, t, par, i, :], bank[1 + 2 * t + par][:, i * TOK:(i + 1) * TOK], ACT.Exp,
                                bias=small[:, 8 + c:9 + c], scale=stats[:, col + t:col + t + 1],
                                accum_out=small[:, 16 + c:17 + c])
                        ins.then_inc(mprob, 1)

            def mem_turned(l):
                for t in range(TB):
                    act.wait_ge(mturn, 4 * l + 2 * t + 1)
                    src = bank[1 + 2 * t][:].rearrange("p (i m s) -> p i m s", i=2, m=2)
                    for i in range(2):
                        ins = A(mpT[:, 0, i, :, t * P:(t + 1) * P], src[:, i], ACT.Copy)
                    ins.then_inc(mturned_a, 1)

            def mem_out_hi(l, b):
                act.wait_ge(mout, l + 1)
                A(mT[0][:, 6:8, :].rearrange("p a b -> p (a b)"), bank[b][:], ACT.Copy).then_inc(mout_hi, 1)

            def main_hi(b, src):
                A(mT[0][:, 2 * b:2 * b + 2, :].rearrange("p a b -> p (a b)"), bank[src][:],
                  ACT.Copy).then_inc(mainT_hi, 1)

            def y_out(banks, last_unit):
                act.wait_ge(weights_used, last_unit + 1)
                for h in range(2):
                    A(x[:, 0, h * 512:(h + 1) * 512], bank[banks[h]][:], ACT.Copy).then_inc(y_act, 1)

            nc.scalar.preload_act_table(ACT.Sqrt)
            act.wait_ge(x_loaded, 16)
            act.wait_ge(gains_ready, 1)
            turned_hi_of(hT[0], 0, 0, (0, 1))
            feed(1)
            turned_hi_of(hT[0], 0, 0, (2, 3))
            squares(x, xn, 2)
            act.wait_ge(mem_loaded, 16)
            squares(memn, squares_of_mem, 0)
            root(0, 4)
            feed(1)
            turned_hi_of(mT[0], 1, 16)
            feed(4)
            scaled_out(z[:, 0, 1536:2048], bank[0][:], U_A0 + 1, 1, 2)
            feed(2)
            kv_out(0, U_KV0 + 1)
            feed(2)
            scaled_out(z[:, 0, 0:512], bank[2][:], U_A1 + 1, 1, 2)
            turned_hi_of(mT[0], 2, 24)
            feed(2)
            scaled_out(z[:, 0, 512:1024], bank[0][:], U_A2 + 1, 1, 2)
            feed(2)
            for t in range(TB):
                act.wait_ge(gate_logits, t + 1)
                A(abs_g[:, t, :], bank[2 + t][:, 0:GQK], ACT.Abs).then_inc(act_chain, 1)
            chain[0] += TB
            act.wait_ge(act_chain, chain[0])
            for t in range(TB):
                A(abs_g[:, t, :], abs_g[:, t, :], ACT.Exp, scale=-1.0).then_inc(act_chain, 1)
            chain[0] += TB
            act.wait_ge(act_chain, chain[0])
            for t in range(TB):
                A(ln_g[:, t, :], abs_g[:, t, :], ACT.Ln, bias=1.0).then_inc(ln_ready, 1)
            kv_out(1, U_KV1 + 1)
            feed(2)
            scaled_out(z[:, 0, 1024:1536], bank[0][:], U_A3 + 1, 1, 2)
            feed(2)
            for t in range(TB):
                act.wait_ge(cum_done, t + 1)
                cum, rem = bank[4 + 2 * t][:, 0:GQK], bank[5 + 2 * t][:, 0:GQK]
                A(ex[0][:, t, :], cum, ACT.Exp).then_inc(gexp, 1)
                A(ex[1][:, t, :], cum, ACT.Exp, scale=-1.0).then_inc(gexp, 1)
                A(ex[2][:, t, :], rem, ACT.Exp).then_inc(gexp, 1)
            chunk_out(qmT[:, 0, :], bank[2][:, 0:TOK], U_AQM)
            feed(1)
            scaled_out(z[:, 0, 2048:A_QM], bank[0][:, 0:A_QM - 2048], U_A4 + 1, 1, 2)

            def qT_out(t):
                act.wait_ge(gturn, 2 * t + 1)
                A(qdT[:, t].rearrange("p h s -> p (h s)"), bank[(5, 7)[t]][0:GDK, :], ACT.Copy).then_inc(gturned_q, 1)

            nc.scalar.preload_act_table(ACT.Exp)
            mem_probs(0, 12, 0)
            act.wait_ge(decay_done, 1)
            for i in range(2):
                A(small[0:GDK, 32 + 4 * i:36 + 4 * i], bank[7 * (1 - i)][0:GDK, 0:GH],
                  ACT.Exp).then_inc(decay_ready, 1)
            qT_out(0)
            mem_probs(0, 12, 1)
            qT_out(1)
            mem_turned(0)
            act.wait_ge(proj_act, 6)
            act.wait_ge(proj_dve, 6)
            for t in range(TB):
                A(z[:, t, A_R:A_QM], z[:, t, A_R:A_QM], ACT.Silu).then_inc(silu_r, 1)
            mem_out_hi(0, 7)
            for t in range(TB):
                act.wait_ge(go, t + 1)
                for b in range(2):
                    for h in range(2):
                        c = 40 + 4 * t + 2 * b + h
                        A(o_squares[:, 2 * b + h, :], bank[GLA_O[t][b]][:, h * GDV:(h + 1) * GDV], ACT.Square,
                          accum_out=small[:, c:c + 1]).then_inc(act_chain, 1)
                chain[0] += GH
                act.wait_ge(act_chain, chain[0])
                A(small[:, 40 + 4 * t:44 + 4 * t], small[:, 40 + 4 * t:44 + 4 * t], ACT.Sqrt, bias=EPS,
                  scale=1.0 / GDV).then_inc(oroot, 1)
            for b in range(3):
                act.wait_ge(mainT, b + 1)
                main_hi(b, 1 + b)
            feed(5)
            nc.scalar.preload_act_table(ACT.Sqrt)
            y_out(OUT_BANKS, U_OUT0 + 3)
            act.wait_ge(y_act, 2)
            act.wait_ge(y_dve, 2)
            root_mean_square(x, xn, 4)
            feed(1)
            turned_hi_of(hT[0], 3, 32)

            def ffn_silu(par, last_unit, m, done):
                act.wait_ge(weights_used, m * 6 + (last_unit + 1))
                if done is not None:
                    act.wait_ge(f_act_ready, done)
                A(f_silu[par][:], bank[4 + 2 * par][:], ACT.Silu).then_inc(f_silu_ready, 1)

            def ffn_hi(par, steps_done):
                act.wait_ge(f_act_ready, steps_done + 1)
                A(f_aT[par][0][:].rearrange("p a b -> p (a b)"), f_act[par][:], ACT.Copy).then_inc(f_hi, 1)

            assert fed[0] == U_FFN + SPLIT, fed
            feed(2)
            ffn_silu(0, U_FFN, 0, None)
            ffn_hi(0, 1)
            n0 = fed[0]
            with act.Fori(0, (F_STEPS - 1) // 2) as i:
                for s in range(2):
                    par = (s + 1) % 2
                    split(n0 + 3 * s, i)
                    split(n0 + 3 * s + 1, i)
                    ffn_silu(par, U_FFN + 2 + 3 * s, i, i * 2 + (s + 1))
                    ffn_hi(par, i * 2 + (s + 2))
                    split(n0 + 3 * s + 2, i)
            fed[0] = n0 + 30
            assert fed[0] == U_B0 - 1 + SPLIT
            y_out(FFN_BANKS, U_B0 - 1)

            turned_hi_of(hT[0], 4, 8)
            feed(1)
            act.wait_ge(y_act, 4)
            act.wait_ge(y_dve, 4)
            root_mean_square(x, xn, 6)
            act.wait_ge(angles, 1)
            A(rope_c[:, 1], rope_c[:, 0], ACT.Sin).then_inc(sincos, 1)
            A(rope_c[:, 2], rope_c[:, 2], ACT.Sin).then_inc(sincos, 1)
            feed(2)
            qk_out(0, bank[0], U_B0 + 1)
            chunk_out(qmT[:, 0, :], bank[2][:, 0:TOK], U_BQM)
            feed(2)
            qk_out(1, bank[5], U_B1 + 1)
            nc.scalar.preload_act_table(ACT.Exp)
            mem_probs(1, 14, 0)
            mem_probs(1, 14, 1)
            scaled_out(v_sb[:, 0, :], bank[7][:, 0:SKV * HD], U_BV, 2, 6)
            for b in (0, 2):
                act.wait_ge(sturn, b + 1)
                A(qkT[:, 2 * b:2 * b + 2, :].rearrange("p a b -> p (a b)"), bank[(5, 6, 7, 0)[b]][:],
                  ACT.Copy).then_inc(sturned_a, 1)
            mem_turned(1)
            mem_out_hi(1, 1)
            for g in range(SH // GROUP):
                act.wait_ge(smax, g + 1)
                for t in range(TB):
                    for n in range(GROUP * g, GROUP * (g + 1)):
                        sc = S[:, n, 0:P] if t == 0 else S[:, n, P:3 * P]
                        c = 2 * GROUP * g + GROUP * t + n % GROUP
                        A(sc, sc, ACT.Exp, bias=swa[:, 1, c:c + 1], accum_out=swa[:, 2, c:c + 1]).then_inc(sprob, 1)
                act.wait_ge(sgap, g + 1)
                cols = swa[:, 3, 2 * GROUP * g:2 * GROUP * (g + 1)]
                A(cols, cols, ACT.Exp).then_inc(ssink, 1)
            for n in range(0, SH, 2):
                act.wait_ge(spturn, n + 1)
                if n >= 4:
                    act.wait_ge(sout, n - 3)
                A(spT[n % 4][:], bank[2][:, 0:3 * P], ACT.Copy).then_inc(spturned_a, 1)
                if n == 6:
                    act.wait_ge(sout, 5)
                    main_hi(0, SWA_O[0])
                if n == 10:
                    act.wait_ge(sout, 9)
                    main_hi(1, SWA_O[1])
            act.wait_ge(sout, SH)
            main_hi(2, SWA_O[2])
            act.dma_start(ffn_gain[:], ffn_norm[1].partition_broadcast(P)).then_inc(ffn_gain_loaded, 16)
            feed(5)
            nc.scalar.preload_act_table(ACT.Sqrt)
            y_out(OUT_BANKS, U_OUT1 + 3)
            act.dma_start(final_gain[:], final_norm.partition_broadcast(P)).then_inc(final_gain_loaded, 16)

            act.wait_ge(y_act, 6)
            act.wait_ge(y_dve, 6)
            root_mean_square(x, xn, 8)
            act.wait_ge(turned, 20 + 1)
            for k in range(2):
                ins = A(xT[:, k, :], bank[4][:, k * TOK:(k + 1) * TOK], ACT.Copy, scale=gains[:, 40 + k:41 + k])
            ins.then_inc(xT_act, 1)
            feed(1)
            act.wait_ge(gap_ready, 1)
            A(route[:, 32:34], route[:, 32:34], ACT.Exp).then_inc(gap_exp, 1)
            assert fed[0] == U_EXP + SPLIT

            def gathered_hi(count):
                for b in range(2):
                    act.wait_ge(gathered, count * 2 + (b - 1))
                    A(hT[0][:, 4 * b:4 * b + 4, 0:P], bank[6 + b][:].rearrange("p (k s) -> p k s", k=4),
                      ACT.Copy).then_inc(gath_hi, 1)

            def down_hi(s):
                act.wait_ge(e_turned, s)
                A(e_aT[0], bank[2][:].rearrange("p (a b) -> p a b", a=4), ACT.Copy).then_inc(e_hi, 1)

            def gate_silu(m, s):
                act.wait_ge(weights_used, m * 6 + (U_EXP + 6))
                act.wait_ge(e_act_ready, s)
                A(e_silu[:], bank[0][:], ACT.Silu).then_inc(e_silu_ready, 1)

            nc.scalar.preload_act_table(ACT.Silu)
            gathered_hi(1)
            feed(2)
            act.wait_ge(routed, 1)
            rounds = act.value_load(rounds_i[0:1, 0:1], min_val=1, max_val=ROUNDS)
            total = act.snap(rounds * NE)
            with act.Fori(0, total) as t:
                steps = act.snap(t * E_STEPS)
                act.wait_ge(weights_used, steps * 6 + (U_EXP + 2))
                A(e_silu[:], bank[0][:], ACT.Silu).then_inc(e_silu_ready, 1)
                split(U_EXP + SPLIT + 2, steps)
                act.wait_ge(pick_turned, t + 1)
                A(pickT[:], bank[2][:, 0:TOK], ACT.Copy).then_inc(pickT_ready, 1)
                split(U_EXP + SPLIT + 3, steps)
                with act.Fori(1, E_STEPS - 1) as j:
                    m, s = act.snap(steps + (j - 1)), act.snap(steps + j)
                    split(U_EXP + 10, m)
                    down_hi(s)
                    split(U_EXP + 11, m)
                    gate_silu(m, s)
                    for i in range(2, 6):
                        split(U_EXP + 10 + i, m)
                m, s = act.snap(steps + (E_STEPS - 2)), act.snap(steps + (E_STEPS - 1))
                down_hi(s)
                gate_silu(m, s)
                for i in range(2):
                    split(U_EXP + 10 + i, m)
                with act.If(total > t + 1):
                    for i in range(2):
                        split(U_EXP + E_UNITS + i, steps)
                down_hi(steps + E_STEPS)
                with act.If(total > t + 1):
                    split(U_EXP + E_UNITS + 2, steps)
                    gathered_hi(t + 2)
                    split(U_EXP + E_UNITS + 3, steps)
                    split(U_EXP + E_UNITS + 4, steps)
                act.wait_ge(weights_used, steps * 6 + (U_EXP + E_UNITS))
                for h in range(2):
                    A(y_s[0][:, h * 512:(h + 1) * 512], bank[3 + h][:], ACT.Copy).then_inc(e_y_hi, 1)
                with act.If(total > t + 1):
                    for i in range(5, 8):
                        split(U_EXP + E_UNITS + i, steps)
                    act.wait_ge(x_added, t * 4 + 4)
                    act.wait_ge(gate_ready, t + 1)
                    for h in range(2):
                        act.wait_ge(scattered, t * 4 + (2 * h + 5))
                        A(y_scaled[2 * h][:], bank[(6, 5)[h]][:], ACT.Copy,
                          scale=gate_now[:, 0:1]).then_inc(y_weighted_act, 1)

            nc.scalar.preload_act_table(ACT.Sqrt)
            for b in range(TB):
                act.wait_ge(x_final, b + 1)
                then(A(xn[:, b, :], x[:, b, :], ACT.Square, accum_out=stats[:, 10 + b:11 + b]))
                root(10 + b, 1)

        @block.vector
        def _(dve):
            V = nc.vector
            MUL, ADD, SUB = ALU.mult, ALU.add, ALU.subtract
            fed = [0]

            def split(n, m=0, words=UNIT):
                for i, half in enumerate(halves_of(words)):
                    dve.wait_ge(weights_hi, m * 12 + (2 * n + i + 1))
                    ins = V.tensor_tensor(wlo[n % SPLIT][:, half], raw[n % RAW][:, half],
                                          whi[n % SPLIT][:, half].bitcast(F32), SUB)
                ins.then_inc(weights_lo, 1)

            def feed(count):
                for _ in range(count):
                    split(fed[0], 0, size(fed[0]))
                    fed[0] += 1

            chain = [0]

            def then(ins):
                chain[0] += 1
                ins.then_inc(dve_chain, 1)
                dve.wait_ge(dve_chain, chain[0])

            def scales(col, mem_col, count):
                dve.wait_ge(root_ready, count)
                then(V.reciprocal(stats[:, col:col + 2], stats[:, col:col + 2]))
                V.tensor_scalar(stats[:, mem_col:mem_col + 2], stats[:, col:col + 2], HD ** -0.5, None,
                                MUL).then_inc(scales_ready, 1)

            def normalise(dst, src, col, count):
                dve.wait_ge(root_ready, count)
                then(V.reciprocal(stats[:, col:col + 2], stats[:, col:col + 2]))
                for t in range(TB):
                    ins = V.tensor_scalar(dst[:, t, :], src[:, t, :], stats[:, col + t:col + t + 1], None, MUL)
                ins.then_inc(normed, 1)

            def turned_lo_of(dst, call, gain_col, banks=range(4)):
                for b in banks:
                    dve.wait_ge(turned_hi, 4 * call + b + 1)
                    for i in range(2):
                        k = 2 * b + i
                        ins = V.scalar_tensor_tensor(
                            dst[1][:, k, :], bank[4 + b][:, i * TOK:(i + 1) * TOK],
                            gains[:, gain_col + k:gain_col + k + 1], dst[0][:, k, :].bitcast(F32), MUL, SUB)
                    ins.then_inc(turned_lo, 1)

            def chunk_out(dst, b, last_unit):
                dve.wait_ge(weights_used, last_unit + 1)
                V.tensor_copy(dst, b).then_inc(proj_dve, 1)

            def scaled_out(dst, b, last_unit, col):
                dve.wait_ge(weights_used, last_unit + 1)
                V.tensor_scalar(dst, b, stats[:, col + 1:col + 2], None, MUL).then_inc(proj_dve, 1)

            def kv_out(l, last_unit):
                dve.wait_ge(weights_used, last_unit + 1)
                for t in range(TB):
                    ins = V.tensor_copy(vm[l][:, t, :], bank[6 + t][:, 0:MEM_W])
                ins.then_inc(kv_dve, 1)

            def qk_out(half, b, last_unit):
                dve.wait_ge(weights_used, last_unit + 1)
                for dst, src in qk_pieces(1, half, b):
                    ins = V.tensor_scalar(dst, src, stats[:, 7:8], None, MUL)
                ins.then_inc(proj_dve, 1)

            def mem_max(l, col, t):
                dve.wait_ge(mscore, 2 * l + t + 1)
                for par in range(2):
                    c = 4 * t + 2 * par
                    V.tensor_reduce(small[:, c:c + 2], bank[1 + 2 * t + par][:].rearrange("p (i s) -> p i s", i=2),
                                    AX.X, ALU.max).then_inc(dve_chain, 1)
                chain[0] += 2
                dve.wait_ge(dve_chain, chain[0])
                V.tensor_scalar(small[:, 8 + 4 * t:12 + 4 * t], small[:, 4 * t:4 * t + 4],
                                stats[:, col + t:col + t + 1], -1.0, MUL, MUL).then_inc(mmax, 1)

            def mem_norm(l, t):
                dve.wait_ge(mprob, 8 * l + 4 * t + 4)
                den = small[:, 16 + 4 * t:20 + 4 * t]
                then(V.reciprocal(den, den))
                probs = mp[:, t].rearrange("p r i s -> p (r i) s")
                V.tensor_tensor(probs, probs, den.unsqueeze(2).broadcast_to([P, 4, TOK]), MUL).then_inc(mnorm, 1)

            def mem_turned(l):
                for t in range(TB):
                    dve.wait_ge(mturn, 4 * l + 2 * t + 2)
                    src = bank[2 + 2 * t][:].rearrange("p (i m s) -> p i m s", i=2, m=2)
                    for i in range(2):
                        ins = V.tensor_copy(mpT[:, 1, i, :, t * P:(t + 1) * P], src[:, i])
                    ins.then_inc(mturned_d, 1)

            def mem_out_lo(l, b):
                dve.wait_ge(mout_hi, l + 1)
                V.tensor_tensor(mT[1][:, 6:8, :].rearrange("p a b -> p (a b)"), bank[b][:],
                                mT[0][:, 6:8, :].bitcast(F32).rearrange("p a b -> p (a b)"), SUB).then_inc(mout_lo, 1)

            def main_lo(l, b, src):
                dve.wait_ge(mainT_hi, 3 * l + b + 1)
                V.tensor_tensor(mT[1][:, 2 * b:2 * b + 2, :].rearrange("p a b -> p (a b)"), bank[src][:],
                                mT[0][:, 2 * b:2 * b + 2, :].bitcast(F32).rearrange("p a b -> p (a b)"),
                                SUB).then_inc(mainT_lo, 1)

            def y_out(banks, last_unit):
                dve.wait_ge(weights_used, last_unit + 1)
                for h in range(2):
                    V.tensor_copy(x[:, 1, h * 512:(h + 1) * 512], bank[banks[2 + h]][:]).then_inc(y_dve, 1)

            dve.wait_ge(gains_turned, 1)
            V.tensor_copy(gains[:], bank[0][:, 0:48]).then_inc(gains_ready, 1)
            turned_lo_of(hT, 0, 0, (0, 1))
            feed(1)
            turned_lo_of(hT, 0, 0, (2, 3))
            scales(2, 12, 1)
            normalise(memn, memn, 0, 1)
            feed(1)
            turned_lo_of(mT, 1, 16)
            feed(4)
            then(V.memset(glrT[:], 1.0))
            scaled_out(z[:, 1, 1536:2048], bank[1][:], U_A0 + 1, 2)
            feed(2)
            kv_out(0, U_KV0 + 1)
            feed(2)
            scaled_out(z[:, 1, 0:512], bank[3][:], U_A1 + 1, 2)
            dve.wait_ge(glr_turned, 1)
            V.tensor_copy(glrT[0:LOWRANK, :], bank[0][0:LOWRANK, 0:TOK]).then_inc(glr_ready, 1)
            turned_lo_of(mT, 2, 24)
            feed(2)
            scaled_out(z[:, 1, 512:1024], bank[1][:], U_A2 + 1, 2)
            feed(2)
            kv_out(1, U_KV1 + 1)
            for t in range(TB):
                dve.wait_ge(ln_ready, t + 1)
                V.scalar_tensor_tensor(la[:, t, :], bank[2 + t][:, 0:GQK], 0.0, ln_g[:, t, :],
                                       ALU.min, SUB).then_inc(la_ready, 1)
            feed(2)
            scaled_out(z[:, 1, 1024:1536], bank[1][:], U_A3 + 1, 2)
            feed(2)
            dve.wait_ge(proj_act, 3)
            dve.wait_ge(proj_dve, 3)
            for t in range(TB):
                q, k = z[:, t, 0:GQK], z[:, t, GQK:2 * GQK]
                dve.wait_ge(gexp, 3 * t + 3)
                V.scalar_tensor_tensor(q, q, GDK ** -0.5, ex[0][:, t, :], MUL, MUL).then_inc(gdec, 1)
                V.tensor_tensor(ex[2][:, t, :], k, ex[2][:, t, :], MUL).then_inc(gdec, 1)
                V.tensor_tensor(k, k, ex[1][:, t, :], MUL).then_inc(gdec, 1)
            chunk_out(qmT[:, 1, :], bank[3][:, 0:TOK], U_AQM)
            feed(1)
            scaled_out(z[:, 1, 2048:A_QM], bank[5][:, 0:A_QM - 2048], U_A4 + 1, 2)
            for t in range(TB):
                mem_max(0, 12, t)
            mem_norm(0, 0)
            for t in range(TB):
                dve.wait_ge(gturn, 2 * t + 2)
                V.tensor_copy(kdT[:, t].rearrange("p h s -> p (h s)"),
                              bank[(6, 0)[t]][0:GDK, :]).then_inc(gturned_k, 1)
            mem_norm(0, 1)
            mem_turned(0)
            for t in range(TB):
                dve.wait_ge(gattn, t + 1)
                V.tensor_tensor(attn[:, t], bank[5 + t][:].rearrange("p (h s) -> p h s", h=GH),
                                causal[:].unsqueeze(1).broadcast_to([P, GH, P]), MUL).then_inc(gattn_ready, 1)
            mem_out_lo(0, 7)
            dve.wait_ge(decay_ready, 2)
            for c in range(3):
                dve.wait_ge(gkv, c + 1)
                if c == 0:
                    for b in range(2):
                        ins = V.tensor_copy(state[0][:, 2 * b:2 * b + 2, :],
                                            bank[GLA_KV[0][b]][0:GDK, 0:2 * GDV].rearrange("p (h v) -> p h v", h=2))
                else:
                    dve.wait_ge(gstate, c)
                    for h in range(GH):
                        d = 32 + 4 * (c - 1) + h
                        ins = V.scalar_tensor_tensor(
                            state[c][:, h, :], state[c - 1][:, h, :], small[0:GDK, d:d + 1],
                            bank[GLA_KV[c][h // 2]][0:GDK, (h % 2) * GDV:(h % 2 + 1) * GDV], MUL, ADD)
                ins.then_inc(gstate, 1)
            for t in range(TB):
                dve.wait_ge(silu_r, t + 1)
                r = z[:, t, A_R:A_QM].rearrange("p (h v) -> p h v", h=GH)
                ins = V.tensor_tensor(r, r, gla_gain[:].unsqueeze(1).broadcast_to([P, GH, GDV]), MUL)
                then(ins)
            for t in range(TB):
                dve.wait_ge(oroot, t + 1)
                c = 40 + 4 * t
                then(V.reciprocal(small[:, c:c + 4], small[:, c:c + 4]))
                for h in range(GH):
                    o = bank[GLA_O[t][h // 2]][:, h % 2 * GDV:(h % 2 + 1) * GDV]
                    ins = V.scalar_tensor_tensor(o_sb[:, t, h, :], o, small[:, c + h:c + h + 1],
                                                 z[:, t, A_R + h * GDV:A_R + (h + 1) * GDV], MUL, MUL)
                ins.then_inc(onorm, 1)
            for b in range(3):
                main_lo(0, b, 1 + b)
            feed(5)
            y_out(OUT_BANKS, U_OUT0 + 3)
            V.sem_inc(f_act_ready, 1)
            normalise(xn, x, 4, 2)
            turned_lo_of(hT, 3, 32)
            feed(1)

            def ffn_act(par, up_unit, m, done):
                dve.wait_ge(weights_used, m * 6 + (up_unit + 1))
                dve.wait_ge(f_silu_ready, done)
                V.tensor_tensor(f_act[par][:], f_silu[par][:], bank[5 + 2 * par][:], MUL).then_inc(f_act_ready, 1)
                dve.wait_ge(f_hi, done)
                V.tensor_tensor(f_aT[par][1][:].rearrange("p a b -> p (a b)"), f_act[par][:],
                                f_aT[par][0][:].bitcast(F32).rearrange("p a b -> p (a b)"), SUB).then_inc(f_lo, 1)

            assert fed[0] == U_FFN + SPLIT, fed
            feed(2)
            ffn_act(0, U_FFN + 1, 0, 1)
            n0 = fed[0]
            with dve.Fori(0, (F_STEPS - 1) // 2) as i:
                for s in range(2):
                    split(n0 + 3 * s, i)
                    split(n0 + 3 * s + 1, i)
                    ffn_act((s + 1) % 2, U_FFN + 3 + 3 * s, i, i * 2 + (s + 2))
                    split(n0 + 3 * s + 2, i)
            fed[0] = n0 + 30
            y_out(FFN_BANKS, U_B0 - 1)

            turned_lo_of(hT, 4, 8)
            feed(1)
            scales(6, 14, 3)
            ang, turn = rope_c[:, 0], rope_c[:, 3]
            freq = ROPE_THETA ** (-np.arange(ROPE_HALF) / ROPE_HALF)
            dve.wait_ge(params_loaded, 16 * 6)
            by_head = swa[:, 0, 0:SH]
            then(V.tensor_copy(by_head.rearrange("p (a j r) -> p a r j", a=2, r=2),
                               sinks[:].rearrange("p (a r j) -> p a r j", a=2, r=2)))
            for t in range(TB):
                ins = V.tensor_copy(sinks_at[:].rearrange("p (g t i) -> p g t i", t=TB, i=GROUP)[:, :, t, :],
                                    by_head.rearrange("p (g i) -> p g i", i=GROUP))
            then(ins)
            then(V.tensor_copy(stats[:, 20:22], pos_i[:]))
            for i in range(ROPE_HALF):
                ins = V.tensor_scalar(ang.rearrange("p (t i) -> p t i", t=TB)[:, :, i:i + 1],
                                      stats[:, 20:22].unsqueeze(2), float(np.float32(freq[i])), None, MUL)
            then(ins)
            magic = 1.5 * 2 ** 23
            then(V.tensor_scalar(turn, ang, 1 / (2 * math.pi), magic, MUL, ADD))
            then(V.tensor_scalar(turn, turn, magic, None, SUB))
            c1 = 6.28125
            c2 = float(np.float32(round((2 * math.pi - c1) * 2 ** 17) / 2 ** 17))
            for c in (c1, c2, 2 * math.pi - c1 - c2):
                then(V.scalar_tensor_tensor(ang, turn, -c, ang, MUL, ADD))
            edge = float(np.nextafter(np.float32(math.pi), np.float32(0)))
            then(V.tensor_scalar(ang, ang, edge, -edge, ALU.min, ALU.max))
            then(V.scalar_tensor_tensor(rope_c[:, 2], ang, -1.0, ang, MUL, ALU.max))
            V.tensor_scalar(rope_c[:, 2], rope_c[:, 2], -1.0, math.pi / 2, MUL, ADD).then_inc(angles, 1)
            feed(2)
            qk_out(0, bank[1], U_B0 + 1)
            chunk_out(qmT[:, 1, :], bank[3][:, 0:TOK], U_BQM)
            feed(2)
            qk_out(1, bank[6], U_B1 + 1)
            dve.wait_ge(sincos, 2)
            dve.wait_ge(proj_act, 9)
            dve.wait_ge(proj_dve, 9)
            for t in range(TB):
                def per_head(a):
                    return a[:, t * 8:t * 8 + 8].unsqueeze(1).broadcast_to([P, SH + SKV, ROPE_HALF])

                sin, cos = per_head(rope_c[:, 1]), per_head(rope_c[:, 2])
                x1, x2 = qk[:, t, :, 0:ROPE_HALF], qk[:, t, :, ROPE_HALF:2 * ROPE_HALF]
                for i, (a, b) in enumerate(((x1, cos), (x2, sin), (x2, cos), (x1, sin))):
                    ins = V.tensor_tensor(rope[i][:, t], a, b, MUL)
                then(ins)
                V.tensor_tensor(x1, rope[0][:, t], rope[1][:, t], SUB)
                ins = V.tensor_tensor(x2, rope[2][:, t], rope[3][:, t], ADD)
            ins.then_inc(roped, 1)
            for t in range(TB):
                mem_max(1, 14, t)
            for t in range(TB):
                mem_norm(1, t)
            scaled_out(v_sb[:, 1, :], bank[0][:, 0:SKV * HD], U_BV, 6)
            for b in (1, 3):
                dve.wait_ge(sturn, b + 1)
                V.tensor_copy(qkT[:, 2 * b:2 * b + 2, :].rearrange("p a b -> p (a b)"),
                              bank[(5, 6, 7, 0)[b]][:]).then_inc(sturned_d, 1)
            mem_turned(1)

            def group_scaled(g):
                for n in range(GROUP * g, GROUP * (g + 1)):
                    dve.wait_ge(sscore, n + 1)
                    V.scalar_tensor_tensor(S[:, n, :], bank[(5, 6, 7, 0)[n % 4]][:, 0:3 * P], HD ** -0.5,
                                           window[:], MUL, ADD).then_inc(sscaled, 1)

            def group_max(g):
                dve.wait_ge(sscaled, GROUP * (g + 1))
                heads, cols = slice(GROUP * g, GROUP * (g + 1)), slice(2 * GROUP * g, 2 * GROUP * (g + 1))
                m = swa[:, 0, cols]
                V.tensor_reduce(m[:, 0:GROUP], S[:, heads, 0:P], AX.X, ALU.max)
                then(V.tensor_reduce(m[:, GROUP:2 * GROUP], S[:, heads, P:3 * P], AX.X, ALU.max))
                then(V.tensor_tensor(m, m, sinks_at[:, cols], ALU.max))
                V.tensor_scalar(swa[:, 1, cols], m, -1.0, None, MUL).then_inc(smax, 1)
                V.tensor_tensor(swa[:, 3, cols], sinks_at[:, cols], m, SUB).then_inc(sgap, 1)

            def group_norm(g):
                dve.wait_ge(sprob, 2 * GROUP * (g + 1))
                dve.wait_ge(ssink, g + 1)
                den = swa[:, 2, 2 * GROUP * g:2 * GROUP * (g + 1)]
                then(V.tensor_tensor(den, den, swa[:, 3, 2 * GROUP * g:2 * GROUP * (g + 1)], ADD))
                then(V.reciprocal(den, den))
                for t in range(TB):
                    sc = S[:, GROUP * g:GROUP * (g + 1), 0:P] if t == 0 else S[:, GROUP * g:GROUP * (g + 1), P:3 * P]
                    d = den[:, GROUP * t:GROUP * (t + 1)].unsqueeze(2).broadcast_to([P, GROUP, P * (t + 1)])
                    ins = V.tensor_tensor(sc, sc, d, MUL)
                ins.then_inc(snorm, 1)

            group_scaled(0)
            group_max(0)
            mem_out_lo(1, 1)
            group_scaled(1)
            group_scaled(2)
            group_max(1)
            group_max(2)
            group_norm(0)
            group_norm(1)
            group_norm(2)
            for n in range(1, SH, 2):
                dve.wait_ge(spturn, n + 1)
                if n >= 4:
                    dve.wait_ge(sout, n - 3)
                V.tensor_copy(spT[n % 4][:], bank[3][:, 0:3 * P]).then_inc(spturned_d, 1)
                if n == 5:
                    main_lo(1, 0, SWA_O[0])
                if n == 9:
                    main_lo(1, 1, SWA_O[1])
            main_lo(1, 2, SWA_O[2])
            feed(5)
            y_out(OUT_BANKS, U_OUT1 + 3)

            for b in (1, 2, 3):
                dve.wait_ge(turned, 20 + b + 1)
                for k in (2 * b, 2 * b + 1):
                    ins = V.tensor_scalar(xT[:, k, :], bank[4 + b][:, (k % 2) * TOK:(k % 2 + 1) * TOK],
                                          gains[:, 40 + k:41 + k], None, MUL)
                ins.then_inc(xT_dve, 1)
            dve.wait_ge(root_ready, 4)
            dve.wait_ge(ffn_gain_loaded, 16)
            then(V.reciprocal(stats[:, 8:10], stats[:, 8:10]))

            def expert_tokens(t):
                V.scalar_tensor_tensor(xn[:, t, :], x[:, t, :], stats[:, 8 + t:9 + t], ffn_gain[:], MUL,
                                       MUL).then_inc(normed, 1)

            expert_tokens(0)
            dve.wait_ge(logits, 1)
            for t in range(TB):
                ins = V.tensor_scalar(route[:, NE * t:NE * (t + 1)], bank[t][:, 0:NE],
                                      stats[:, 8 + t:9 + t], None, MUL)
            then(ins)
            for t in range(TB):
                ins = V.max(route[:, 16 + 8 * t:24 + 8 * t], route[:, NE * t:NE * (t + 1)])
            then(ins)
            for t in range(TB):
                ins = V.max_index(route_u[:, t, :], route[:, 16 + 8 * t:24 + 8 * t], route[:, NE * t:NE * (t + 1)])
            top = route[:, 16:32].rearrange("p (t i) -> p t i", t=TB)
            then(ins)
            then(V.tensor_copy(route[:, 40:44].rearrange("p (t i) -> p t i", t=TB), route_u[:, :, 0:2]))
            one_hot = route[:, 160:192].rearrange("p (t i e) -> p t i e", t=TB, i=2)
            for t in range(TB):
                ins = V.tensor_tensor(one_hot[:, t], iota[:, 0:NE].unsqueeze(1).broadcast_to([P, 2, NE]),
                                      route[:, 40 + 2 * t:42 + 2 * t].unsqueeze(2).broadcast_to([P, 2, NE]),
                                      ALU.is_equal)
            then(ins)
            chosen = route[:, 64:64 + TB * NE].rearrange("p (t e) -> p t e", t=TB)
            V.tensor_tensor(chosen, one_hot[:, :, 0], one_hot[:, :, 1], ADD).then_inc(mask_ready, 1)
            V.tensor_tensor(route[:, 32:34].unsqueeze(2), top[:, :, 1:2], top[:, :, 0:1], SUB).then_inc(gap_ready, 1)
            expert_tokens(1)

            def slots(r):
                for t in range(TB):
                    c = 96 + 16 * t + NE * r
                    ins = V.scalar_tensor_tensor(route[:, c:c + 8], bank[2 + t][:, 0:NE], 1.0 - P * r,
                                                 route[:, 64 + NE * t:72 + NE * t], ADD, MUL)
                then(ins)
                by_block = route[:, 96:128].rearrange("p (t r e) -> p t r e", t=TB, r=ROUNDS)[:, :, r]
                then(V.tensor_scalar(by_block, by_block, 1.0, None, SUB))

            def make_pick(t):
                for b in range(TB):
                    c = t + (96 + 16 * b)
                    slot = route[:, c:c + 1] if isinstance(t, int) else route[:, bass.ds(c, 1)]
                    ins = V.tensor_scalar(pick[:, b, :], iota[:], slot, None, ALU.is_equal)
                ins.then_inc(pick_made, 1)

            dve.wait_ge(ranks, 1)
            slots(0)
            make_pick(0)
            slots(1)
            then(V.tensor_reduce(route[0:1, 38:39], bank[4][0:1, 0:NE], AX.X, ALU.max))
            V.tensor_scalar(rounds_i[:], route[0:1, 38:39], float(P), 1.0, ALU.is_gt, ADD).then_inc(routed, 1)
            feed(1)
            dve.wait_ge(gap_exp, 1)
            then(V.tensor_scalar(route[:, 34:36], route[:, 32:34], 1.0, None, ADD))
            then(V.reciprocal(route[:, 34:36], route[:, 34:36]))
            then(V.tensor_tensor(route[:, 36:38], route[:, 34:36], route[:, 32:34], MUL))
            for t in range(TB):
                c = 160 + 16 * t
                ins = V.tensor_scalar(route[:, c:c + 8], route[:, c:c + 8], route[:, 34 + t:35 + t], None, MUL)
            then(ins)
            for t in range(TB):
                c = 160 + 16 * t
                for r in range(ROUNDS):
                    g = 128 + 16 * t + NE * r
                    ins = V.scalar_tensor_tensor(route[:, g:g + 8], route[:, c + 8:c + 16], route[:, 36 + t:37 + t],
                                                 route[:, c:c + 8], MUL, ADD)
            then(ins)

            def gathered_lo(count):
                for b in range(2):
                    dve.wait_ge(gath_hi, count * 2 + (b - 1))
                    V.tensor_tensor(hT[1][:, 4 * b:4 * b + 4, 0:P], bank[6 + b][:].rearrange("p (k s) -> p k s", k=4),
                                    hT[0][:, 4 * b:4 * b + 4, 0:P].bitcast(F32), SUB).then_inc(gath_lo, 1)

            def activate(s, up_unit, m):
                dve.wait_ge(weights_used, m * 6 + (up_unit + 1))
                dve.wait_ge(e_silu_ready, s)
                V.tensor_tensor(e_act[:], e_silu[:], bank[1][:], MUL).then_inc(e_act_ready, 1)

            def down_lo(s):
                dve.wait_ge(e_hi, s)
                V.tensor_tensor(e_aT[1], bank[2][:].rearrange("p (a b) -> p a b", a=4),
                                e_aT[0].bitcast(F32), SUB).then_inc(e_lo, 1)

            def output_lo(t, h):
                dve.wait_ge(e_y_hi, t * 2 + (h + 1))
                V.tensor_tensor(y_s[1][:, h * 512:(h + 1) * 512], bank[3 + h][:],
                                y_s[0][:, h * 512:(h + 1) * 512].bitcast(F32), SUB).then_inc(e_y_lo, 1)

            V.sem_inc(y_weighted_act, 1)
            V.sem_inc(y_weighted_dve, 1)
            V.sem_inc(x_added, 4)
            V.sem_inc(scattered, 4)
            dve.wait_ge(routed, 1)
            assert fed[0] == U_EXP + SPLIT
            gathered_lo(1)
            feed(2)
            rounds = dve.value_load(rounds_i[0:1, 0:1], min_val=1, max_val=ROUNDS)
            total = dve.snap(rounds * NE)
            with dve.Fori(0, total) as t:
                steps = dve.snap(t * E_STEPS)
                split(U_EXP + SPLIT + 2, steps)
                activate(steps + 1, U_EXP + 3, steps)
                split(U_EXP + SPLIT + 3, steps)
                with dve.Fori(1, E_STEPS - 1) as j:
                    m, s = dve.snap(steps + (j - 1)), dve.snap(steps + j)
                    split(U_EXP + 10, m)
                    down_lo(s)
                    for i in range(1, 4):
                        split(U_EXP + 10 + i, m)
                    activate(s + 1, U_EXP + 7, m)
                    for i in range(4, 6):
                        split(U_EXP + 10 + i, m)
                m, s = dve.snap(steps + (E_STEPS - 2)), dve.snap(steps + (E_STEPS - 1))
                down_lo(s)
                split(U_EXP + 10, m)
                split(U_EXP + 11, m)
                activate(s + 1, U_EXP + 7, m)
                with dve.If(total > t + 1):
                    make_pick(t + 1)
                    for i in range(2):
                        split(U_EXP + E_UNITS + i, steps)
                down_lo(steps + E_STEPS)
                with dve.If(total > t + 1):
                    split(U_EXP + E_UNITS + 2, steps)
                    gathered_lo(t + 2)
                    split(U_EXP + E_UNITS + 3, steps)
                    split(U_EXP + E_UNITS + 4, steps)
                for b in range(TB):
                    ins = V.tensor_copy(gate_now[:, b:b + 1], route[:, bass.ds(t + (128 + 16 * b), 1)])
                ins.then_inc(gate_ready, 1)
                output_lo(t, 0)
                with dve.If(total > t + 1):
                    split(U_EXP + E_UNITS + 5, steps)
                output_lo(t, 1)
                with dve.If(total > t + 1):
                    split(U_EXP + E_UNITS + 6, steps)
                    split(U_EXP + E_UNITS + 7, steps)
                    dve.wait_ge(x_added, t * 4 + 4)
                    for h in range(2):
                        dve.wait_ge(scattered, t * 4 + (2 * h + 6))
                        V.tensor_scalar(y_scaled[2 * h + 1][:], bank[(7, 2)[h]][:], gate_now[:, 1:2],
                                        None, MUL).then_inc(y_weighted_dve, 1)
            dve.wait_ge(gate_ready, total)
            dve.wait_ge(x_added, total * 4)
            for b in range(TB):
                for h in range(2):
                    dve.wait_ge(scattered, total * 4 + (2 * h + b + 1))
                    xo = x[:, b, h * 512:(h + 1) * 512]
                    ins = V.scalar_tensor_tensor(xo, bank[(6, 7, 5, 2)[2 * h + b]][:], gate_now[:, b:b + 1], xo,
                                                 MUL, ADD)
                ins.then_inc(x_final, 1)
            dve.wait_ge(final_gain_loaded, 16)
            for b in range(TB):
                dve.wait_ge(root_ready, 5 + b)
                then(V.reciprocal(stats[:, 10 + b:11 + b], stats[:, 10 + b:11 + b]))
                V.scalar_tensor_tensor(out_sb[:, b, :], x[:, b, :], stats[:, 10 + b:11 + b], final_gain[:],
                                       MUL, MUL).then_inc(normed, 1)


_INS = ["x", "mem", "positions", "mix_norm", "w_in_a", "gla_gate_w", "gla_gate_b", "gla_out_norm", "w_in_b",
        "swa_sinks", "mem_norm", "w_mem_kv", "w_out", "ffn_norm", "ffn_w_gate_up", "ffn_w_down", "router_w",
        "exp_w_gate_up", "exp_w_down", "final_norm"]


def kernel(**inputs):
    import numpy as _np
    import concourse.bacc as _bacc
    from concourse import mybir as _mybir
    from concourse.bass_utils import run_bass_kernel_spmd as _run

    nc = _bacc.Bacc("TRN2", target_bir_lowering=False, num_devices=1)
    arrays, args = {}, []
    for name in _INS:
        a = _np.ascontiguousarray(inputs[name])
        arrays[f"in_{name}"] = a
        args.append(nc.dram_tensor(f"in_{name}", a.shape, _mybir.dt.from_np(a.dtype), kind="ExternalInput").ap())
    res = nc.dram_tensor("out_x", (1, TOK, D), F32, kind="ExternalOutput").ap()
    build(nc, *args, res)
    r = _run(nc, [arrays], core_ids=[0])
    return r.results[0]["out_x"]
```
